# Optimizing a Trainium2 kernel written in Bass

```python
import math
import jax, jax.numpy as jnp
from jax import lax
import numpy as np

D_MODEL = 1024
BATCH = 1
SEQ = 256
DEPTH = 2

ATTN_HEADS = 8
HEAD_DIM = 64
ATTN_WIDTH = ATTN_HEADS * HEAD_DIM
LRU_BLOCKS = 8
LRU_BLOCK_W = 64
LRU_WIDTH = LRU_BLOCKS * LRU_BLOCK_W
MIX_WIDTH = ATTN_WIDTH + LRU_WIDTH
IN_COLS = 3 * ATTN_WIDTH + 2 * LRU_WIDTH

DILATED_PAIRS = ((128, 1), (512, 4), (2048, 16))
Q_BLOCK = 128
ROT_DIM = HEAD_DIM // 4
ROPE_THETA = 500000.0
ATTN_SCALE = 1.0 / math.sqrt(HEAD_DIM)
NEG_INF = -1e30

CONV_W = 4
LRU_C = 8.0

D_FF = 3584
N_EXPERTS = 8
TOP_K = 2
N_DENSE = (DEPTH + 1) // 2
N_MOE = DEPTH // 2

RMS_EPS = 1e-6

kernel_name = "hymba_dilated_rglru_moe_trunk"

def rmsnorm(x, g):
    xf = x.astype(jnp.float32)
    var = jnp.mean(xf * xf, axis=-1, keepdims=True)
    return (xf * lax.rsqrt(var + RMS_EPS) * g.astype(jnp.float32)).astype(x.dtype)

def partial_rotary(t, positions):
    half = ROT_DIM // 2
    inv_freq = ROPE_THETA ** (-jnp.arange(half, dtype=jnp.float32) / half)
    ang = positions.astype(jnp.float32)[..., None] * inv_freq
    cos = jnp.cos(ang)[:, :, None, :]
    sin = jnp.sin(ang)[:, :, None, :]
    tf = t.astype(jnp.float32)
    t1 = tf[..., :half]
    t2 = tf[..., half:ROT_DIM]
    out = jnp.concatenate([t1 * cos - t2 * sin, t2 * cos + t1 * sin, tf[..., ROT_DIM:]], axis=-1)
    return out.astype(t.dtype)

def dilated_branch(q, k, v, window, dilation):
    B, S, H, Dh = q.shape
    L = S // dilation
    w_sub = window // dilation
    nb = -(-L // Q_BLOCK)
    Lp = nb * Q_BLOCK

    def to_sub(t):
        t = t.reshape(B, L, dilation, H, Dh).transpose(0, 2, 1, 3, 4)
        return jnp.pad(t, ((0, 0), (0, 0), (0, Lp - L), (0, 0), (0, 0)))

    qs, ks, vs = to_sub(q), to_sub(k), to_sub(v)
    blk = (B, dilation, nb, Q_BLOCK, H, Dh)
    qb = qs.reshape(blk)

    def band_keys(t):
        prev = jnp.pad(t, ((0, 0), (0, 0), (Q_BLOCK, 0), (0, 0), (0, 0)))[:, :, :Lp]
        return jnp.concatenate([prev.reshape(blk), t.reshape(blk)], axis=3)

    kb, vb = band_keys(ks), band_keys(vs)

    s = jnp.einsum('bgnqhd,bgnkhd->bgnhqk', qb, kb) * ATTN_SCALE
    qi = jnp.arange(Q_BLOCK)[:, None]
    kj = jnp.arange(2 * Q_BLOCK)[None, :]
    delta = Q_BLOCK + qi - kj
    band = (delta >= 0) & (delta <= w_sub)
    blk_id = jnp.arange(nb)[:, None, None]
    valid = band[None] & ((blk_id > 0) | (kj[None] >= Q_BLOCK))
    s = jnp.where(valid[None, None, :, None], s, NEG_INF)

    m = jnp.max(s, axis=-1, keepdims=True)
    p = jnp.exp(s - m)
    den = jnp.sum(p, axis=-1)
    o = jnp.einsum('bgnhqk,bgnkhd->bgnqhd', p, vb)
    o = o / jnp.swapaxes(den, -1, -2)[..., None]
    lse = jnp.swapaxes(m[..., 0] + jnp.log(den), -1, -2)

    o = o.reshape(B, dilation, Lp, H, Dh)[:, :, :L].transpose(0, 2, 1, 3, 4).reshape(B, S, H, Dh)
    lse = lse.reshape(B, dilation, Lp, H)[:, :, :L].transpose(0, 2, 1, 3).reshape(B, S, H)
    return o, lse

def dilated_mixture_attention(q, k, v):
    qf, kf, vf = q.astype(jnp.float32), k.astype(jnp.float32), v.astype(jnp.float32)
    outs, lses = [], []
    for window, dilation in DILATED_PAIRS:
        o, lse = dilated_branch(qf, kf, vf, window, dilation)
        outs.append(o)
        lses.append(lse)
    w = jax.nn.softmax(jnp.stack(lses, axis=0), axis=0)
    o = jnp.sum(w[..., None] * jnp.stack(outs, axis=0), axis=0)
    return o.astype(q.dtype)

def causal_dwconv(u, w, b):
    S = u.shape[1]
    up = jnp.pad(u, ((0, 0), (CONV_W - 1, 0), (0, 0)))
    y = b
    for tap in range(CONV_W):
        y = y + up[:, tap:tap + S] * w[tap]
    return y

def rg_lru(u, w_r, b_r, w_i, b_i, lam):
    B, S, _ = u.shape
    uf = u.astype(jnp.float32)
    ub = uf.reshape(B, S, LRU_BLOCKS, LRU_BLOCK_W)
    r = jax.nn.sigmoid(jnp.einsum('bsgi,gij->bsgj', ub, w_r.astype(jnp.float32)).reshape(B, S, -1)
                       + b_r.astype(jnp.float32))
    i = jax.nn.sigmoid(jnp.einsum('bsgi,gij->bsgj', ub, w_i.astype(jnp.float32)).reshape(B, S, -1)
                       + b_i.astype(jnp.float32))
    log_a = -LRU_C * r * jax.nn.softplus(-lam.astype(jnp.float32))
    a = jnp.exp(log_a)
    mult = jnp.sqrt(-jnp.expm1(2.0 * log_a))
    bterm = mult * i * uf

    def combine(left, right):
        a1, b1 = left
        a2, b2 = right
        return a1 * a2, a2 * b1 + b2

    _, h = lax.associative_scan(combine, (a, bterm), axis=1)
    return h.astype(u.dtype)

def swiglu(t, wg, wu, wd):
    return (jax.nn.silu(t @ wg) * (t @ wu)) @ wd

def moe_ffn(h, router_w, wg, wu, wd):
    B, S, D = h.shape
    t = h.reshape(-1, D)
    logits = t.astype(jnp.float32) @ router_w.astype(jnp.float32)
    vals, idx = lax.top_k(logits, TOP_K)
    probs = jax.nn.softmax(vals, axis=-1)
    gates = jnp.sum(jax.nn.one_hot(idx, N_EXPERTS, dtype=jnp.float32) * probs[..., None], axis=1)
    y = jnp.zeros(t.shape, jnp.float32)
    for e in range(N_EXPERTS):
        y = y + gates[:, e:e + 1] * swiglu(t, wg[e], wu[e], wd[e]).astype(jnp.float32)
    return y.astype(h.dtype).reshape(B, S, D)

def setup_inputs(seed: int = 0) -> dict:
    key = jax.random.key(seed)
    ks = jax.random.split(key, 26)
    f32 = jnp.float32

    def nrm(k, shape, fan_in):
        return jax.random.normal(k, shape, f32) * (fan_in ** -0.5)

    def gain(k, shape):
        return 1.0 + 0.02 * jax.random.normal(k, shape, f32)

    x = jax.random.normal(ks[0], (BATCH, SEQ, D_MODEL), f32)
    offset = jax.random.randint(ks[1], (BATCH, 1), 0, 4096, dtype=jnp.int32)
    positions = (offset + jnp.arange(SEQ, dtype=jnp.int32)[None, :]).astype(jnp.int32)

    u = jax.random.uniform(ks[2], (DEPTH, LRU_WIDTH), f32, 0.9, 0.999)
    a0 = u ** (1.0 / LRU_C)
    lru_lambda = jnp.log(a0) - jnp.log1p(-a0)

    return {
        "x": x,
        "positions": positions,
        "pre_mix_g": gain(ks[3], (DEPTH, D_MODEL)),
        "w_in": nrm(ks[4], (DEPTH, D_MODEL, IN_COLS), D_MODEL),
        "conv_w": nrm(ks[5], (DEPTH, CONV_W, LRU_WIDTH), CONV_W),
        "conv_b": 0.02 * jax.random.normal(ks[6], (DEPTH, LRU_WIDTH), f32),
        "w_rgate": nrm(ks[7], (DEPTH, LRU_BLOCKS, LRU_BLOCK_W, LRU_BLOCK_W), LRU_BLOCK_W),
        "b_rgate": 0.02 * jax.random.normal(ks[8], (DEPTH, LRU_WIDTH), f32),
        "w_igate": nrm(ks[9], (DEPTH, LRU_BLOCKS, LRU_BLOCK_W, LRU_BLOCK_W), LRU_BLOCK_W),
        "b_igate": 0.02 * jax.random.normal(ks[10], (DEPTH, LRU_WIDTH), f32),
        "lru_lambda": lru_lambda,
        "attn_out_g": gain(ks[11], (DEPTH, ATTN_WIDTH)),
        "lru_out_g": gain(ks[12], (DEPTH, LRU_WIDTH)),
        "w_out": nrm(ks[13], (DEPTH, MIX_WIDTH, D_MODEL), MIX_WIDTH),
        "post_mix_g": gain(ks[14], (DEPTH, D_MODEL)),
        "pre_ffn_g": gain(ks[15], (DEPTH, D_MODEL)),
        "post_ffn_g": gain(ks[16], (DEPTH, D_MODEL)),
        "dense_w_gate": nrm(ks[17], (N_DENSE, D_MODEL, D_FF), D_MODEL),
        "dense_w_up": nrm(ks[18], (N_DENSE, D_MODEL, D_FF), D_MODEL),
        "dense_w_down": nrm(ks[19], (N_DENSE, D_FF, D_MODEL), D_FF),
        "router_w": nrm(ks[20], (N_MOE, D_MODEL, N_EXPERTS), D_MODEL),
        "moe_w_gate": nrm(ks[21], (N_MOE, N_EXPERTS, D_MODEL, D_FF), D_MODEL),
        "moe_w_up": nrm(ks[22], (N_MOE, N_EXPERTS, D_MODEL, D_FF), D_MODEL),
        "moe_w_down": nrm(ks[23], (N_MOE, N_EXPERTS, D_FF, D_MODEL), D_FF),
    }

def reference(x, positions, pre_mix_g, w_in, conv_w, conv_b, w_rgate, b_rgate, w_igate, b_igate,
              lru_lambda, attn_out_g, lru_out_g, w_out, post_mix_g, pre_ffn_g, post_ffn_g,
              dense_w_gate, dense_w_up, dense_w_down, router_w, moe_w_gate, moe_w_up, moe_w_down):
    B, S, _ = x.shape
    c1 = ATTN_WIDTH
    c2 = 2 * ATTN_WIDTH
    c3 = 3 * ATTN_WIDTH
    c4 = 3 * ATTN_WIDTH + LRU_WIDTH
    for l in range(DEPTH):
        h = rmsnorm(x, pre_mix_g[l])
        z = h @ w_in[l]
        q = z[..., :c1].reshape(B, S, ATTN_HEADS, HEAD_DIM)
        k = z[..., c1:c2].reshape(B, S, ATTN_HEADS, HEAD_DIM)
        v = z[..., c2:c3].reshape(B, S, ATTN_HEADS, HEAD_DIM)
        u = z[..., c3:c4]
        g = z[..., c4:]

        q = partial_rotary(q, positions)
        k = partial_rotary(k, positions)
        attn = dilated_mixture_attention(q, k, v).reshape(B, S, ATTN_WIDTH)

        uc = causal_dwconv(u, conv_w[l], conv_b[l])
        rec = rg_lru(uc, w_rgate[l], b_rgate[l], w_igate[l], b_igate[l], lru_lambda[l])
        rec = jax.nn.gelu(g) * rec

        mixed = jnp.concatenate([rmsnorm(attn, attn_out_g[l]), rmsnorm(rec, lru_out_g[l])], axis=-1)
        x = x + rmsnorm(mixed @ w_out[l], post_mix_g[l])

        h = rmsnorm(x, pre_ffn_g[l])
        if l % 2 == 0:
            j = l // 2
            f = swiglu(h, dense_w_gate[j], dense_w_up[j], dense_w_down[j])
        else:
            j = l // 2
            f = moe_ffn(h, router_w[j], moe_w_gate[j], moe_w_up[j], moe_w_down[j])
        x = x + rmsnorm(f, post_ffn_g[l])
    return x


_drawn_inputs = setup_inputs


def setup_inputs(seed=0):
    import zlib

    import numpy as np

    out = dict(_drawn_inputs(seed))
    spreads = {}
    factors = {'b_rgate': 8.0, 'b_igate': 8.0}
    for name, (base, spread) in spreads.items():
        noise = np.random.default_rng([zlib.crc32(name.encode()), seed]).standard_normal(out[name].shape)
        drawn = base * np.exp(spread * noise) if base else spread * noise
        out[name] = __import__('jax').numpy.asarray(drawn.astype(out[name].dtype))
    for name, factor in factors.items():
        out[name] = (out[name] * factor).astype(out[name].dtype)
    return out
```

```python
from contextlib import ExitStack
import math

import numpy as np
import concourse.bass as bass
from concourse import mybir

F32 = mybir.dt.float32
I32 = mybir.dt.int32
ALU = mybir.AluOpType
ACT = mybir.ActivationFunctionType
AX_X = mybir.AxisListType.X

P = 128
T = 256
TT = T // P
D = 1024
DK = D // P
LAYERS = 2
HEADS, DH = 8, 64
AW = HEADS * DH
LW = 512
LJ = LW // P
ROT = DH // 4
HALF = ROT // 2
TAPS = 4
FF = 3584
EXPERTS = 8
EPS = 1e-6
NEG = -1e30
SCALE = 1.0 / math.sqrt(DH)

UCOLS = 2048
FC = UCOLS // DK
NCH = FF // FC
FT = FF // P
FPC = FC // P
RING = 14

C = 112
NCHUNK = -(-T // C)
NCAND = (NCHUNK - 1) * EXPERTS
NEXTRA = (2 * T - 1) // C
NITEM = EXPERTS + NEXTRA

IN_ORDER = [6, 7, 8, 9, 0, 1, 2, 3, 4, 5]
OUT_ORDER = [2, 3, 0, 1]


def ffn_units():
    order = [("gate", 0), ("up", 0)]
    for c in range(1, NCH):
        order += [("gate", c), ("up", c), ("down", c - 1)]
    return order + [("down", NCH - 1)]


FFN_UNITS = ffn_units()
NFU = len(FFN_UNITS)
PRE = []
for _l in range(LAYERS):
    PRE += [("in", _l, i) for i in range(len(IN_ORDER))]
    PRE += [("out", _l, i) for i in range(len(OUT_ORDER))]
    if _l == 0:
        PRE += [(kind, 0, c) for kind, c in FFN_UNITS]
NPRE = len(PRE)
assert NPRE % RING == 0 and NFU % RING == 0
PRE_AT = {u: n for n, u in enumerate(PRE)}
FFN_AT = {u: n for n, u in enumerate(FFN_UNITS)}

PARAM_COLS = [("pre_mix_g", LAYERS * DK), ("pre_ffn_g", LAYERS * DK), ("conv_w", LAYERS * LJ * TAPS),
              ("conv_b", LAYERS * LJ), ("b_rgate", LAYERS * LJ), ("b_igate", LAYERS * LJ),
              ("lru_lambda", LAYERS * LJ), ("attn_out_g", LAYERS * LJ), ("lru_out_g", LAYERS * LJ),
              ("router_w", DK * EXPERTS)]
CONST_COLS = [("ident", P), ("tri", P), ("iota", P), ("mask", T), ("inv_freq", HALF),
              ("first", EXPERTS), ("chunk0", NCAND), ("cand_e", NCAND)]


def columns(table):
    at, out = 0, {}
    for name, n in table:
        out[name] = (at, at + n)
        at += n
    return out, at


PAR, NPAR = columns(PARAM_COLS)
CON, NCON = columns(CONST_COLS)


def constants():
    c = np.zeros((P, NCON), np.float32)
    p = np.arange(P)[:, None]

    def put(name, v):
        a, b = CON[name]
        c[:, a:b] = v

    put("ident", p == np.arange(P)[None, :])
    put("tri", p <= np.arange(P)[None, :])
    put("iota", np.arange(P)[None, :])
    delta = p + P - np.arange(T)[None, :]
    count = ((delta >= 0) & (delta <= 128)) * 1
    count = count + ((delta >= 0) & (delta % 4 == 0)) + ((delta >= 0) & (delta % 16 == 0))
    put("mask", np.where(count > 0, np.log(np.maximum(count, 1)) / SCALE, NEG))
    put("inv_freq", 500000.0 ** (-np.arange(HALF) / HALF))
    put("first", EXPERTS - np.arange(EXPERTS)[None, :])
    put("chunk0", (np.arange(NCAND) // EXPERTS + 1)[None, :] * C)
    put("cand_e", (np.arange(NCAND) % EXPERTS)[None, :])
    return c


PRE_MIX, ATTN, POST_MIX, PRE_FFN, POST_FFN = range(5)


def stat(layer, which, tt):
    return (layer * 5 + which) * TT + tt


def build(nc, x, positions, consts, params, gains, gate_blocks, in_units, out_units,
          dense_gate, dense_up, dense_down, moe_gate, moe_up, moe_down, out):
    with ExitStack() as ctx:
        def sb(name, shape, dt=F32):
            return ctx.enter_context(nc.sbuf_tensor(name, shape, dt))

        def sem(name):
            return ctx.enter_context(nc.semaphore(name))

        ring = sb("ring", [P, RING, UCOLS])
        xs = sb("xs", [P, TT, D])
        hn = sb("hn", [P, TT, D])
        hT = sb("hT", [P, DK, T])
        gain = sb("gain", [P, 2, D])
        qk = sb("qk", [P, TT, 2 * AW])
        qkT = sb("qkT", [P, 2 * AW // P, T])
        u_pad = sb("u_pad", [P, LJ, T + TAPS - 1])
        lru_y = sb("lru_y", [P, LJ, T])
        lru_a = sb("lru_a", [P, LJ, T])
        lru_b = sb("lru_b", [P, LJ, T])
        lru_d = sb("lru_d", [P, LJ, T])
        lru_g = sb("lru_g", [P, LJ, T])
        blocks = sb("blocks", [P, 2, LJ, P])
        masked = sb("masked", [P, 2, 3 * P])
        probs = sb("probs", [P, 2, 3 * P])
        probsT = sb("probsT", [P, 2, 3 * P])
        silu = sb("silu", [P, 2, T])
        con = sb("con", [P, NCON])
        par = sb("par", [P, NPAR])
        ones = sb("ones", [P, P])
        pos_i = sb("pos_i", [P, TT], I32)
        small = sb("small", [P, 4, TT, HALF])
        cs = sb("cs", [P, 2, TT, HALF])
        rot = sb("rot", [P, 4, 2 * HEADS, HALF])
        sp = sb("sp", [P, 4, LAYERS * LJ])
        negmax = sb("negmax", [P, 2, 4])
        den = sb("den", [P, HEADS, TT])
        rden = sb("rden", [P, HEADS, TT])
        ssq = sb("ssq", [P, 10 * LAYERS])
        ms = sb("ms", [P, 10 * LAYERS])
        rstd = sb("rstd", [P, 10 * LAYERS])
        mhalf = sb("mhalf", [P, 1])
        eps = sb("eps", [P, 1])
        lg = sb("lg", [P, 6, TT, EXPERTS])
        top = sb("top", [P, 6, TT])
        gates = sb("gates", [P, TT, EXPERTS])
        mask_te = sb("mask_te", [P, TT, EXPERTS])
        slot = sb("slot", [P, TT, EXPERTS])
        cnt = sb("cnt", [P, EXPERTS])
        cand = sb("cand", [P, 6, NCAND])
        item_slot = sb("item_slot", [P, TT, NITEM + 1])
        item_gate = sb("item_gate", [P, TT, NITEM + 1])
        extra_f = sb("extra_f", [P, 1 + NEXTRA])
        extra_i = sb("extra_i", [P, 1 + NEXTRA], I32)

        v_at = hn[:, :, 0:AW]
        o_at = hn[:, :, AW:2 * AW]
        mixA = qk[:, 0, :].rearrange("p (k t) -> p k t", k=LJ)
        junk = lru_b[:, :, :].rearrange("p a b -> p (a b)")
        act = lru_a
        heT = lru_b[:, :, :].rearrange("p a b -> p (a b)")[:, 0:DK * C].rearrange("p (k c) -> p k c", k=DK)
        ye = lru_d[:, :, :].rearrange("p a b -> p (a b)")
        g_flat = lru_g[:, :, :].rearrange("p a b -> p (a b)")
        pick = g_flat[:, 0:TT * C].rearrange("p (t c) -> p t c", t=TT)
        pick_g = g_flat[:, TT * C:2 * TT * C].rearrange("p (t c) -> p t c", t=TT)
        pick_gT = g_flat[:, 2 * TT * C:2 * TT * C + T]
        y_sum = qkT[:, :, :].rearrange("p (a b) t -> p a (b t)", a=TT)

        psum = ctx.enter_context(nc.psum_tensor("psum", [P, 8, 512], F32))
        ps = [psum[:, i, :] for i in range(8)]

        def cc(name, a=None, b=None):
            lo, hi = CON[name]
            return con[:, lo + (a or 0):(lo + b) if b is not None else hi]

        def pc(name, i):
            lo, _ = PAR[name]
            return par[:, lo + i:lo + i + 1]

        ident = cc("ident")

        x_loaded = [sem(f"x_loaded{i}") for i in range(TT)]
        consts_loaded = sem("consts_loaded")
        params_loaded = sem("params_loaded")
        pos_loaded = sem("pos_loaded")
        gain_loaded = sem("gain_loaded")
        blocks_loaded = [sem(f"blocks_loaded{i}") for i in range(2)]
        unit_loaded = [sem(f"unit_loaded{i}") for i in range(RING)]
        cleared = sem("cleared")
        sumsq_ready = sem("sumsq_ready")
        pool_chain = sem("pool_chain")
        rstd_ready = sem("rstd_ready")
        hn_ready = sem("hn_ready")
        norm_tr = sem("norm_tr")
        hT_dve = sem("hT_dve")
        hT_act = sem("hT_act")
        angles_ready = sem("angles_ready")
        cs_ready = sem("cs_ready")
        explam_ready = sem("explam_ready")
        sp_ready = sem("sp_ready")
        u_ready = sem("u_ready")
        u_evac = sem("u_evac")
        conv_ready = sem("conv_ready")
        g_ready = sem("g_ready")
        gelu_ready = sem("gelu_ready")
        gates_mm = sem("gates_mm")
        sigmoids = sem("sigmoids")
        tau_ready = sem("tau_ready")
        rho_ready = sem("rho_ready")
        sqrt_ready = sem("sqrt_ready")
        rec_ready = sem("rec_ready")
        rec2_ready = sem("rec2_ready")
        ssR_ready = sem("ssR_ready")
        rmsR_ready = sem("rmsR_ready")
        mixR_ready = sem("mixR_ready")
        qkv_ready = sem("qkv_ready")
        v_evac = sem("v_evac")
        rot_ready = sem("rot_ready")
        qk_tr = sem("qk_tr")
        qkT_act = sem("qkT_act")
        qkT_dve = sem("qkT_dve")
        scores_ready = sem("scores_ready")
        masked_ready = sem("masked_ready")
        probs_ready = sem("probs_ready")
        probs_tr = sem("probs_tr")
        probsT_ready = sem("probsT_ready")
        pv_done = sem("pv_done")
        o_ready = sem("o_ready")
        on_ready = sem("on_ready")
        o_tr = sem("o_tr")
        mixA_dve = sem("mixA_dve")
        mixA_act = sem("mixA_act")
        wout_used = sem("wout_used")
        m_ready = sem("m_ready")
        x_updated = sem("x_updated")
        gu_ready = sem("gu_ready")
        silu_ready = sem("silu_ready")
        act_ready = sem("act_ready")
        down_step = sem("down_step")
        f_ready = sem("f_ready")
        logits_ready = sem("logits_ready")
        top_diff = sem("top_diff")
        exp_diff = sem("exp_diff")
        mask_ready = sem("mask_ready")
        slots_mm = sem("slots_mm")
        routed = sem("routed")
        pick_ready = sem("pick_ready")
        pick_g_ready = sem("pick_g_ready")
        pick_tr = sem("pick_tr")
        pick_gT_ready = sem("pick_gT_ready")
        gathered = sem("gathered")
        heT_ready = sem("heT_ready")
        ye_dve = sem("ye_dve")
        ye_act = sem("ye_act")
        comb_ready = sem("comb_ready")
        comb_added = sem("comb_added")
        dve_chain = sem("dve_chain")
        dve_item = sem("dve_item")
        stored = sem("stored")

        F_MOE = FT

        def slot_of(n):
            return ring[:, n % RING, :]

        block = ctx.enter_context(nc.Block())

        @block.sync
        def _(sync):
            sync.dma_start(xs[:, 0, :], x[0]).then_inc(x_loaded[0], 16)
            sync.dma_start(xs[:, 1, :], x[1]).then_inc(x_loaded[1], 16)
            sync.dma_start(con[:, :], consts).then_inc(consts_loaded, 16)
            sync.dma_start(par[:, :], params).then_inc(params_loaded, 16)

            def wait_used(n):
                kind, layer, i = PRE[n]
                if kind == "in" and i < 2:
                    sync.wait_ge(u_ready, 2 * layer + i + 1)
                elif kind == "in" and i < 4:
                    sync.wait_ge(g_ready, 2 * layer + i - 1)
                elif kind == "in":
                    sync.wait_ge(qkv_ready, 6 * layer + i - 4 + 1)
                elif kind == "out" and i < 3:
                    sync.wait_ge(wout_used, 3 * layer + i + 1)
                elif kind == "out":
                    sync.wait_ge(m_ready, TT * (layer + 1))
                elif kind == "down":
                    sync.wait_ge(down_step, FPC * (i + 1))
                else:
                    sync.wait_ge(gu_ready, FPC * (i + 1))

            source = {"gate": dense_gate, "up": dense_up, "down": dense_down}
            for n, (kind, layer, i) in enumerate(PRE):
                if n >= RING:
                    wait_used(n - RING)
                if kind == "in":
                    src = in_units[layer, IN_ORDER[i]]
                elif kind == "out":
                    src = out_units[layer, OUT_ORDER[i]]
                else:
                    src = source[kind][i]
                sync.dma_start(slot_of(n), src).then_inc(unit_loaded[n % RING], 16)

            source_e = {"gate": moe_gate, "up": moe_up, "down": moe_down}

            def item_loads(item, expert, first=False):
                for n, (kind, c) in enumerate(FFN_UNITS):
                    if n < RING and first:
                        wait_used(NPRE - RING + n)
                    else:
                        k, cu = FFN_UNITS[(n - RING) % NFU]
                        back = item if n >= RING else item - 1
                        s = down_step if k == "down" else gu_ready
                        sync.wait_ge(s, back * FT + (F_MOE + FPC * (cu + 1)))
                    sync.dma_start(slot_of(n), source_e[kind][expert, c]).then_inc(unit_loaded[n % RING], 16)

            item_loads(0, 0, first=True)
            with sync.Fori(1, EXPERTS) as item:
                item_loads(item, item)
            sync.wait_ge(routed, 1)
            extras = sync.value_load(extra_i[0:1, 0:1], min_val=0, max_val=NEXTRA)
            with sync.If(extras > 0):
                with sync.Fori(0, extras) as j:
                    expert = sync.value_load(extra_i[0:1, bass.ds(j + 1, 1)], min_val=0, max_val=EXPERTS - 1)
                    item_loads(j + EXPERTS, expert)

            for tt in range(TT):
                sync.wait_ge(x_updated, TT * (2 * LAYERS - 1) + tt + 1)
                sync.dma_start(out[tt], xs[:, tt, :]).then_inc(stored, 16)
            sync.wait_ge(stored, 16 * TT)

        @block.gpsimd
        def _(pool):
            pool.memset(mhalf[:, :], -0.5).then_inc(pool_chain, 1)
            n = 1
            for layer in range(LAYERS):
                for which in (PRE_MIX, ATTN, POST_MIX, PRE_FFN, POST_FFN):
                    width = AW if which == ATTN else D
                    for tt in range(TT):
                        r = stat(layer, which, tt)
                        pool.wait_ge(sumsq_ready, r + 1)
                        pool.tensor_scalar(ms[:, r:r + 1], ssq[:, r:r + 1], 1.0 / width, EPS,
                                           ALU.mult, ALU.add).then_inc(pool_chain, 1)
                        n += 1
                        pool.wait_ge(pool_chain, n)
                        pool.tensor_tensor(rstd[:, r:r + 1], ms[:, r:r + 1], mhalf[:, :],
                                           ALU.pow).then_inc(rstd_ready, 1)

        @block.tensor
        def _(pe):
            def loaded(n):
                pe.wait_ge(unit_loaded[n % RING], 16 * (n // RING + 1))

            def norm_transposes(layer, which):
                n = 2 * layer + (which == PRE_FFN)
                pe.wait_ge(hn_ready, TT * (n + 1))
                for kp in range(DK // 2):
                    if kp >= 2:
                        pe.wait_ge(hT_act if kp % 2 else hT_dve, 2 * n + 1)
                    for k in (2 * kp, 2 * kp + 1):
                        for tt in range(TT):
                            mm = pe.transpose(ps[6 + kp % 2][:, (k % 2) * T + tt * P:(k % 2) * T + tt * P + P],
                                              hn[:, tt, k * P:(k + 1) * P], ident)
                    mm.then_inc(norm_tr, 1)

            def wait_hT(n):
                pe.wait_ge(hT_dve, 2 * (n + 1))
                pe.wait_ge(hT_act, 2 * (n + 1))

            def channels(layer, i, bank, ready):
                n = PRE_AT[("in", layer, i)]
                loaded(n)
                w = slot_of(n).rearrange("p (k f) -> p k f", k=DK)
                for j in range(2):
                    for k in range(DK):
                        mm = pe.matmul(ps[bank][:, j * T:(j + 1) * T], w[:, k, j * P:(j + 1) * P], hT[:, k, :],
                                       start=(k == 0), stop=(k == DK - 1))
                mm.then_inc(ready, 1)

            def tokens(layer, m, bank):
                n = PRE_AT[("in", layer, m + 4)]
                loaded(n)
                w = slot_of(n).rearrange("p (k f) -> p k f", k=DK)
                for tt in range(TT):
                    for k in range(DK):
                        mm = pe.matmul(ps[bank][:, tt * 256:(tt + 1) * 256], hT[:, k, tt * P:(tt + 1) * P],
                                       w[:, k, :], start=(k == 0), stop=(k == DK - 1))
                mm.then_inc(qkv_ready, 1)

            def mixer(layer):
                norm_transposes(layer, PRE_MIX)
                wait_hT(2 * layer)
                for i in range(2):
                    channels(layer, i, i, u_ready)
                for i in range(2):
                    channels(layer, 2 + i, 2 + i, g_ready)
                tokens(layer, 0, 6)
                for h in range(2):
                    pe.wait_ge(blocks_loaded[h], 16 * (layer + 1))
                for j in range(LJ):
                    pe.wait_ge(conv_ready, LJ * layer + j + 1)
                    if j >= 2:
                        pe.wait_ge(sigmoids, LJ * layer + j - 1)
                    for g in range(2):
                        mm = pe.matmul(ps[4 + j % 2][:, g * T:(g + 1) * T], blocks[:, g, j, :], lru_y[:, j, :],
                                       start=True, stop=True)
                    mm.then_inc(gates_mm, 1)
                tokens(layer, 1, 7)
                pe.wait_ge(u_evac, LJ * layer + LJ)
                tokens(layer, 2, 0)
                tokens(layer, 3, 1)
                pe.wait_ge(gelu_ready, LJ * layer + LJ)
                tokens(layer, 4, 2)
                tokens(layer, 5, 3)
                pe.wait_ge(rec2_ready, layer + 1)
                for j in range(LJ):
                    mm = pe.matmul(ps[5][:, 0:T], ones[:, :], lru_d[:, j, :], start=(j == 0), stop=(j == LJ - 1))
                mm.then_inc(ssR_ready, 1)
                pe.wait_ge(rot_ready, TT * (layer + 1))
                for b, bank in enumerate((6, 7, 0, 1)):
                    for t in (2 * b, 2 * b + 1):
                        for tt in range(TT):
                            mm = pe.transpose(ps[bank][:, (t % 2) * T + tt * P:(t % 2) * T + tt * P + P],
                                              qk[:, tt, t * P:(t + 1) * P], ident)
                    mm.then_inc(qk_tr, 1)
                pe.wait_ge(qkT_act, 2 * (layer + 1))
                pe.wait_ge(qkT_dve, 2 * (layer + 1))
                pe.wait_ge(v_evac, 2 * (layer + 1))

                def scores(h):
                    if h >= 2:
                        pe.wait_ge(masked_ready, HEADS * layer + h - 1)
                    lo = (h % 2) * DH
                    q = qkT[lo:lo + DH, h // 2, :]
                    k = qkT[lo:lo + DH, LJ + h // 2, :]
                    pe.matmul(ps[h % 2][:, 0:P], q[:, 0:P], k[:, 0:P], start=True, stop=True)
                    pe.matmul(ps[h % 2][:, P:3 * P], q[:, P:2 * P], k[:, 0:2 * P],
                              start=True, stop=True).then_inc(scores_ready, 1)

                def turn(h):
                    pe.wait_ge(probs_ready, HEADS * layer + h + 1)
                    if h >= 2:
                        pe.wait_ge(probsT_ready, HEADS * layer + h - 1)
                    for b in range(3):
                        mm = pe.transpose(ps[2 + h % 2][:, b * P:(b + 1) * P], probs[:, h % 2, b * P:(b + 1) * P], ident)
                    mm.then_inc(probs_tr, 1)

                def weigh(h):
                    pe.wait_ge(probsT_ready, HEADS * layer + h + 1)
                    cols = slice(h * DH, (h + 1) * DH)
                    pT = probsT[:, h % 2, :]
                    pe.matmul(ps[6][:, cols], pT[:, 0:P], v_at[:, 0, cols], start=True, stop=True)
                    pe.matmul(ps[7][:, cols], pT[:, P:2 * P], v_at[:, 0, cols], start=True, stop=False)
                    pe.matmul(ps[7][:, cols], pT[:, 2 * P:3 * P], v_at[:, 1, cols],
                              start=False, stop=True).then_inc(pv_done, 1)

                for h in range(HEADS + 2):
                    if h < HEADS:
                        scores(h)
                    if 1 <= h <= HEADS:
                        turn(h - 1)
                    if h >= 2:
                        weigh(h - 2)

                pe.wait_ge(mixR_ready, layer + 1)
                for i in range(2):
                    n = PRE_AT[("out", layer, i)]
                    loaded(n)
                    w = slot_of(n).rearrange("p (k d) -> p k d", k=2)
                    for k in range(2):
                        for tt in range(TT):
                            for half in range(2):
                                mm = pe.matmul(ps[2 + 2 * tt + half][:, :], lru_y[:, 2 * i + k, tt * P:(tt + 1) * P],
                                               w[:, k, half * 512:(half + 1) * 512],
                                               start=(i == 0 and k == 0), stop=False)
                    mm.then_inc(wout_used, 1)
                pe.wait_ge(on_ready, TT * (layer + 1))
                for b in range(2):
                    for k in (2 * b, 2 * b + 1):
                        for tt in range(TT):
                            mm = pe.transpose(ps[b][:, (k % 2) * T + tt * P:(k % 2) * T + tt * P + P],
                                              o_at[:, tt, k * P:(k + 1) * P], ident)
                    mm.then_inc(o_tr, 1)
                pe.wait_ge(mixA_dve, layer + 1)
                pe.wait_ge(mixA_act, layer + 1)
                for tt in range(TT):
                    for k in range(LJ):
                        n = PRE_AT[("out", layer, 2 + k // 2)]
                        if tt == 0 and k % 2 == 0:
                            loaded(n)
                        w = slot_of(n).rearrange("p (k d) -> p k d", k=2)
                        for half in range(2):
                            mm = pe.matmul(ps[2 + 2 * tt + half][:, :], mixA[:, k, tt * P:(tt + 1) * P],
                                           w[:, k % 2, half * 512:(half + 1) * 512],
                                           start=False, stop=(k == LJ - 1))
                        if tt == 1 and k == 1:
                            mm.then_inc(wout_used, 1)
                    mm.then_inc(m_ready, 1)

            def gate_up(ft, base, wait_unit, at, rhs, width):
                c, f = ft // FPC, ft % FPC
                for g, kind in enumerate(("gate", "up")):
                    n = at(kind, c)
                    if f == 0:
                        wait_unit(n)
                    if g == 0:
                        if wait_bank(base, ft):
                            pe.wait_ge(act_ready, base + (ft - 1))
                    w = slot_of(n).rearrange("p (k f) -> p k f", k=DK)
                    for k in range(DK):
                        mm = pe.matmul(ps[ft % 2][:, g * T:g * T + width], w[:, k, f * P:(f + 1) * P], rhs(k),
                                       start=(k == 0), stop=(k == DK - 1))
                mm.then_inc(gu_ready, 1)

            def wait_bank(base, ft):
                return not (type(base) is int and base + ft < 2)

            def dense():
                norm_transposes(0, PRE_FFN)
                wait_hT(1)

                def at(kind, c):
                    return PRE_AT[(kind, 0, c)]

                def down(ft):
                    c, f = ft // FPC, ft % FPC
                    pe.wait_ge(act_ready, ft + 1)
                    n = at("down", c)
                    if f == 0:
                        loaded(n)
                    w = slot_of(n).rearrange("p (j d) -> p j d", j=FPC)
                    for tt in range(TT):
                        for half in range(2):
                            mm = pe.matmul(ps[2 + 2 * tt + half][:, :], act[:, ft % 4, tt * P:(tt + 1) * P],
                                           w[:, f, half * 512:(half + 1) * 512], start=(ft == 0), stop=(ft == FT - 1))
                    mm.then_inc(down_step, 1)

                for c in range(NCH + 1):
                    if c < NCH:
                        for f in range(FPC):
                            gate_up(c * FPC + f, 0, loaded, at, lambda k: hT[:, k, :], T)
                    if c >= 1:
                        for f in range(FPC):
                            down((c - 1) * FPC + f)

            mixer(0)
            dense()
            mixer(1)

            norm_transposes(1, PRE_FFN)
            wait_hT(3)
            pe.wait_ge(params_loaded, 16)
            lo, _ = PAR["router_w"]
            for tt in range(TT):
                for k in range(DK):
                    mm = pe.matmul(ps[0][:, tt * EXPERTS:(tt + 1) * EXPERTS], hT[:, k, tt * P:(tt + 1) * P],
                                   par[:, lo + k * EXPERTS:lo + (k + 1) * EXPERTS],
                                   start=(k == 0), stop=(k == DK - 1))
            mm.then_inc(logits_ready, 1)
            pe.wait_ge(mask_ready, 1)
            pe.matmul(ps[1][:, 0:EXPERTS], cc("tri"), mask_te[:, 0, :], start=True, stop=True)
            pe.matmul(ps[1][:, EXPERTS:2 * EXPERTS], ones[:, :], mask_te[:, 0, :], start=True, stop=False)
            pe.matmul(ps[1][:, EXPERTS:2 * EXPERTS], cc("tri"), mask_te[:, 1, :], start=False, stop=True)
            pe.matmul(ps[1][:, 2 * EXPERTS:3 * EXPERTS], ones[:, :], mask_te[:, 0, :], start=True, stop=False)
            pe.matmul(ps[1][:, 2 * EXPERTS:3 * EXPERTS], ones[:, :], mask_te[:, 1, :],
                      start=False, stop=True).then_inc(slots_mm, 1)

            def gather():
                for b in range(2):
                    for k in range(4):
                        for tt in range(TT):
                            mm = pe.matmul(ps[6 + b][:, k * C:(k + 1) * C],
                                           hn[:, tt, (4 * b + k) * P:(4 * b + k + 1) * P], pick[:, tt, :],
                                           start=(tt == 0), stop=(tt == TT - 1))
                    mm.then_inc(gathered, 1)

            pe.wait_ge(pick_ready, 1)
            gather()

            pe.wait_ge(routed, 1)
            extras = pe.value_load(extra_i[0:1, 0:1], min_val=0, max_val=NEXTRA)
            with pe.Fori(0, extras + EXPERTS) as item:
                base = item * FT + F_MOE

                def wait_unit(n):
                    pe.wait_ge(unit_loaded[n % RING], item * (16 * NFU // RING) + 16 * ((NPRE + n) // RING + 1))

                def at(kind, c):
                    return FFN_AT[(kind, c)]

                def down(ft):
                    c, f = ft // FPC, ft % FPC
                    pe.wait_ge(act_ready, base + (ft + 1))
                    n = at("down", c)
                    if f == 0:
                        wait_unit(n)
                    w = slot_of(n).rearrange("p (j d) -> p j d", j=FPC)
                    for half in range(2):
                        mm = pe.matmul(ps[2 + half][0:C, :], act[:, ft % 4, 0:C],
                                       w[:, f, half * 512:(half + 1) * 512], start=(ft == 0), stop=(ft == FT - 1))
                    mm.then_inc(down_step, 1)

                pe.wait_ge(heT_ready, item * 2 + 2)
                for c in range(NCH + 1):
                    if c < NCH:
                        for f in range(FPC):
                            gate_up(c * FPC + f, base, wait_unit, at, lambda k: heT[:, k, :], C)
                    if c >= 1:
                        for f in range(FPC):
                            down((c - 1) * FPC + f)
                    if c == 5:
                        pe.wait_ge(pick_g_ready, item + 1)
                        pe.wait_ge(comb_added, item * 4 + 1)
                        for tt in range(TT):
                            mm = pe.transpose(ps[4][0:C, tt * P:(tt + 1) * P], pick_g[:, tt, :], ident)
                        mm.then_inc(pick_tr, 1)
                pe.wait_ge(pick_ready, item + 2)
                gather()
                pe.wait_ge(pick_gT_ready, item + 1)
                pe.wait_ge(ye_dve, item + 1)
                pe.wait_ge(ye_act, item + 1)
                for o in range(4):
                    tt, half = o // 2, o % 2
                    if o >= 2:
                        pe.wait_ge(comb_added, item * 4 + o)
                    pe.matmul(ps[4 + o % 2][:, :], pick_gT[0:C, tt * P:(tt + 1) * P],
                              ye[0:C, half * 512:(half + 1) * 512], start=True, stop=True).then_inc(comb_ready, 1)

        @block.scalar
        def _(act_e):
            for h in range(2):
                act_e.wait_ge(cleared, 2)
                act_e.dma_start(blocks[h * 64:(h + 1) * 64, :, :, h * 64:(h + 1) * 64],
                                gate_blocks[0, h]).then_inc(blocks_loaded[h], 16)
            act_e.dma_start(pos_i[:, :], positions).then_inc(pos_loaded, 16)
            act_e.dma_start(gain[:, :, :], gains[0:1].partition_broadcast(P)).then_inc(gain_loaded, 16)

            def sumsq(r, rows):
                if r >= 1:
                    act_e.wait_ge(sumsq_ready, r)
                n = rows.free_size()
                act_e.activation(junk[:, 0:n], rows, ACT.Square, accum_out=ssq[:, r:r + 1]).then_inc(sumsq_ready, 1)

            def sumsq_x(layer, which):
                for tt in range(TT):
                    s = 2 * layer + (which == PRE_FFN)
                    if s == 0:
                        act_e.wait_ge(x_loaded[tt], 16)
                    else:
                        act_e.wait_ge(x_updated, TT * (s - 1) + tt + 1)
                    sumsq(stat(layer, which, tt), xs[:, tt, :])

            def hT_half(layer, which):
                n = 2 * layer + (which == PRE_FFN)
                name = "pre_ffn_g" if which == PRE_FFN else "pre_mix_g"
                for kp in (1, 3):
                    act_e.wait_ge(norm_tr, 4 * n + kp + 1)
                    for k in (2 * kp, 2 * kp + 1):
                        ins = act_e.activation(hT[:, k, :], ps[7][:, (k % 2) * T:(k % 2 + 1) * T], ACT.Identity,
                                               scale=pc(name, layer * DK + k))
                    ins.then_inc(hT_act, 1)

            sumsq_x(0, PRE_MIX)
            act_e.wait_ge(params_loaded, 16)
            act_e.wait_ge(angles_ready, 1)
            act_e.activation(cs[:, :, :, :], small[:, 2:4, :, :], ACT.Sin).then_inc(cs_ready, 1)
            act_e.wait_ge(explam_ready, 1)
            act_e.activation(sp[:, 1, :], sp[:, 0, :], ACT.Exp, scale=-1.0).then_inc(explam_ready, 1)

            def mixer(layer):
                hT_half(layer, PRE_MIX)
                for j in range(LJ):
                    act_e.wait_ge(u_ready, 2 * layer + j // 2 + 1)
                    act_e.activation(u_pad[:, j, TAPS - 1:], ps[j // 2][:, (j % 2) * T:(j % 2 + 1) * T],
                                     ACT.Copy).then_inc(u_evac, 1)
                for j in range(LJ):
                    act_e.wait_ge(g_ready, 2 * layer + j // 2 + 1)
                    act_e.activation(lru_g[:, j, :], ps[2 + j // 2][:, (j % 2) * T:(j % 2 + 1) * T],
                                     ACT.Gelu_apprx_tanh).then_inc(gelu_ready, 1)
                act_e.wait_ge(sp_ready, 1)
                for j in range(LJ):
                    act_e.wait_ge(gates_mm, LJ * layer + j + 1)
                    bank = ps[4 + j % 2]
                    act_e.activation(lru_a[:, j, :], bank[:, 0:T], ACT.Sigmoid, bias=pc("b_rgate", layer * LJ + j))
                    act_e.activation(lru_b[:, j, :], bank[:, T:2 * T], ACT.Sigmoid,
                                     bias=pc("b_igate", layer * LJ + j)).then_inc(sigmoids, 1)
                act_e.wait_ge(sigmoids, LJ * (layer + 1))
                for j in range(LJ):
                    act_e.activation(lru_a[:, j, :], lru_a[:, j, :], ACT.Tanh,
                                     scale=sp[:, 3, layer * LJ + j:layer * LJ + j + 1]).then_inc(tau_ready, 1)
                act_e.wait_ge(rho_ready, layer + 1)
                act_e.activation(lru_a[:, :, :], lru_a[:, :, :], ACT.Sqrt).then_inc(sqrt_ready, 1)
                act_e.wait_ge(rec_ready, layer + 1)
                act_e.activation(lru_d[:, :, :], lru_y[:, :, :], ACT.Square).then_inc(rec2_ready, 1)
                act_e.wait_ge(ssR_ready, layer + 1)
                act_e.activation(lru_b[:, 0, :], ps[5][:, 0:T], ACT.Sqrt, bias=eps[:, :],
                                 scale=1.0 / LW).then_inc(rmsR_ready, 1)
                for i, (b, bank) in enumerate(((0, 6), (2, 0))):
                    act_e.wait_ge(qk_tr, 4 * layer + b + 1)
                    act_e.activation(qkT[:, 2 * b:2 * b + 2, :], ps[bank][:, :].rearrange("p (a t) -> p a t", a=2),
                                     ACT.Copy).then_inc(qkT_act, 1)
                for h in range(HEADS):
                    act_e.wait_ge(masked_ready, HEADS * layer + h + 1)
                    for tt, cols in enumerate((slice(0, P), slice(P, 3 * P))):
                        ins = act_e.activation(probs[:, h % 2, cols], masked[:, h % 2, cols], ACT.Exp, scale=SCALE,
                                               bias=negmax[:, h % 2, 2 + tt:3 + tt],
                                               accum_out=den[:, h, tt:tt + 1])
                    ins.then_inc(probs_ready, 1)
                for tt in range(TT):
                    act_e.wait_ge(o_ready, TT * layer + tt + 1)
                    sumsq(stat(layer, ATTN, tt), o_at[:, tt, :])
                act_e.wait_ge(o_tr, 2 * layer + 2)
                for k in (2, 3):
                    ins = act_e.activation(mixA[:, k, :], ps[1][:, (k % 2) * T:(k % 2 + 1) * T], ACT.Identity,
                                           scale=pc("attn_out_g", layer * LJ + k))
                ins.then_inc(mixA_act, 1)
                for tt in range(TT):
                    act_e.wait_ge(m_ready, TT * layer + tt + 1)
                    sumsq(stat(layer, POST_MIX, tt), psum[:, 2 + 2 * tt:4 + 2 * tt, :].rearrange("p a b -> p (a b)"))
                sumsq_x(layer, PRE_FFN)
                hT_half(layer, PRE_FFN)

            mixer(0)
            for ft in range(FT):
                act_e.wait_ge(gu_ready, ft + 1)
                act_e.activation(silu[:, ft % 2, :], ps[ft % 2][:, 0:T], ACT.Silu).then_inc(silu_ready, 1)
            act_e.wait_ge(down_step, FT)
            for tt in range(TT):
                sumsq(stat(0, POST_FFN, tt), psum[:, 2 + 2 * tt:4 + 2 * tt, :].rearrange("p a b -> p (a b)"))
            sumsq_x(1, PRE_MIX)
            act_e.dma_start(gain[:, :, :], gains[1:2].partition_broadcast(P)).then_inc(gain_loaded, 16)
            for h in range(2):
                act_e.dma_start(blocks[h * 64:(h + 1) * 64, :, :, h * 64:(h + 1) * 64],
                                gate_blocks[1, h]).then_inc(blocks_loaded[h], 16)
            mixer(1)

            act_e.wait_ge(top_diff, 1)
            act_e.activation(top[:, 3, :], top[:, 2, :], ACT.Exp).then_inc(exp_diff, 1)
            act_e.wait_ge(routed, 1)
            extras = act_e.value_load(extra_i[0:1, 0:1], min_val=0, max_val=NEXTRA)
            with act_e.Fori(0, extras + EXPERTS) as item:
                base = item * FT + F_MOE
                for ft in range(FT):
                    act_e.wait_ge(gu_ready, base + (ft + 1))
                    act_e.activation(silu[:, ft % 2, 0:C], ps[ft % 2][:, 0:C], ACT.Silu).then_inc(silu_ready, 1)
                    if ft == 14:
                        act_e.wait_ge(pick_tr, item + 1)
                        act_e.activation(pick_gT[0:C, :], ps[4][0:C, 0:T], ACT.Copy).then_inc(pick_gT_ready, 1)
                act_e.wait_ge(down_step, base + FT)
                act_e.activation(ye[0:C, 512:D], ps[3][0:C, :], ACT.Copy).then_inc(ye_act, 1)
            n_items = extras + EXPERTS
            act_e.wait_ge(comb_added, n_items * 4 + 1)
            for tt in range(TT):
                sumsq(stat(1, POST_FFN, tt), y_sum[:, tt, :])

        @block.vector
        def _(dve):
            links = [0]

            def link(ins):
                links[0] += 1
                ins.then_inc(dve_chain, 1)
                dve.wait_ge(dve_chain, links[0])

            dve.memset(ones[:, :], 1.0).then_inc(cleared, 1)
            dve.memset(blocks[:, :, :, :], 0.0).then_inc(cleared, 1)
            dve.memset(eps[:, :], EPS)
            link(dve.memset(u_pad[:, :, 0:TAPS - 1], 0.0))

            dve.wait_ge(pos_loaded, 16)
            dve.wait_ge(consts_loaded, 16)
            link(dve.tensor_copy(rot[:, 3, 0, 0:TT], pos_i[:, :]))
            for tt in range(TT):
                link(dve.tensor_scalar(small[:, 0, tt, :], cc("inv_freq"), rot[:, 3, 0, tt:tt + 1], None, ALU.mult))
            magic = 12582912.0
            link(dve.tensor_scalar(small[:, 1, :, :], small[:, 0, :, :], 1.0 / (2 * math.pi), None, ALU.mult))
            link(dve.tensor_scalar(small[:, 1, :, :], small[:, 1, :, :], magic, None, ALU.add))
            link(dve.tensor_scalar(small[:, 1, :, :], small[:, 1, :, :], magic, None, ALU.subtract))
            c1 = 6.28125
            c2 = 0.0019350051879882812
            c3 = 2 * math.pi - c1 - c2
            for c in (c1, c2, c3):
                link(dve.scalar_tensor_tensor(out=small[:, 0, :, :], in0=small[:, 1, :, :], scalar=-c,
                                              in1=small[:, 0, :, :], op0=ALU.mult, op1=ALU.add))
            lim = 3.1415925
            link(dve.tensor_scalar(small[:, 2, :, :], small[:, 0, :, :], -lim, lim, ALU.max, ALU.min))
            link(dve.tensor_scalar(small[:, 0, :, :], small[:, 0, :, :], math.pi / 2, None, ALU.add))
            link(dve.tensor_scalar(small[:, 1, :, :], small[:, 0, :, :], math.pi, -2 * math.pi, ALU.is_gt, ALU.mult))
            link(dve.tensor_tensor(small[:, 0, :, :], small[:, 0, :, :], small[:, 1, :, :], ALU.add))
            dve.tensor_scalar(small[:, 3, :, :], small[:, 0, :, :], -lim, lim, ALU.max,
                              ALU.min).then_inc(angles_ready, 1)

            dve.wait_ge(params_loaded, 16)
            la, lb = PAR["lru_lambda"]
            lam = par[:, la:lb]
            dve.scalar_tensor_tensor(out=sp[:, 0, :], in0=lam, scalar=-1.0, in1=lam, op0=ALU.mult,
                                     op1=ALU.max).then_inc(explam_ready, 1)

            def softplus():
                dve.wait_ge(explam_ready, 2)
                link(dve.tensor_scalar(sp[:, 0, :], sp[:, 1, :], 2.0, None, ALU.add))
                link(dve.reciprocal(sp[:, 0, :], sp[:, 0, :]))
                link(dve.tensor_tensor(sp[:, 0, :], sp[:, 0, :], sp[:, 1, :], ALU.mult))
                link(dve.tensor_tensor(sp[:, 1, :], sp[:, 0, :], sp[:, 0, :], ALU.mult))
                link(dve.tensor_scalar(sp[:, 2, :], sp[:, 1, :], 1.0 / 17, None, ALU.mult))
                for m in (15, 13, 11, 9, 7, 5, 3):
                    link(dve.scalar_tensor_tensor(out=sp[:, 2, :], in0=sp[:, 2, :], scalar=1.0 / m, in1=sp[:, 1, :],
                                                  op0=ALU.add, op1=ALU.mult))
                link(dve.scalar_tensor_tensor(out=sp[:, 2, :], in0=sp[:, 2, :], scalar=1.0, in1=sp[:, 0, :],
                                              op0=ALU.add, op1=ALU.mult))
                link(dve.tensor_scalar(sp[:, 1, :], lam, -1.0, 0.0, ALU.mult, ALU.max))
                link(dve.tensor_scalar(sp[:, 1, :], sp[:, 1, :], 4.0, None, ALU.mult))
                dve.scalar_tensor_tensor(out=sp[:, 3, :], in0=sp[:, 2, :], scalar=8.0, in1=sp[:, 1, :],
                                         op0=ALU.mult, op1=ALU.add).then_inc(sp_ready, 1)

            def normalise(layer, which):
                n = 2 * layer + (which == PRE_FFN)
                name = "pre_ffn_g" if which == PRE_FFN else "pre_mix_g"
                for tt in range(TT):
                    r = stat(layer, which, tt)
                    dve.wait_ge(rstd_ready, r + 1)
                    dve.tensor_scalar(hn[:, tt, :], xs[:, tt, :], rstd[:, r:r + 1], None,
                                      ALU.mult).then_inc(hn_ready, 1)
                for kp in (0, 2):
                    dve.wait_ge(norm_tr, 4 * n + kp + 1)
                    for k in (2 * kp, 2 * kp + 1):
                        ins = dve.tensor_scalar(hT[:, k, :], ps[6][:, (k % 2) * T:(k % 2 + 1) * T],
                                                pc(name, layer * DK + k), None, ALU.mult)
                    ins.then_inc(hT_dve, 1)

            def post_norm(layer, which, ready, src):
                s = 2 * layer + (which == POST_FFN)
                dve.wait_ge(gain_loaded, 16 * (layer + 1))
                for tt in range(TT):
                    r = stat(layer, which, tt)
                    dve.wait_ge(rstd_ready, r + 1)
                    g = int(which == POST_FFN)
                    for half in range(2):
                        cols = slice(half * 512, (half + 1) * 512)
                        ins = dve.scalar_tensor_tensor(out=hn[:, tt, cols], in0=src(tt, half), scalar=rstd[:, r:r + 1],
                                                       in1=gain[:, g, cols], op0=ALU.mult, op1=ALU.mult)
                    link(ins)
                    dve.tensor_tensor(xs[:, tt, :], xs[:, tt, :], hn[:, tt, :], ALU.add).then_inc(x_updated, 1)

            def from_banks(tt, half):
                return ps[2 + 2 * tt + half][:, :]

            def rotate(layer, tt):
                heads = qk[:, tt, :].rearrange("p (h d) -> p h d", d=DH)
                t1, t2 = heads[:, :, 0:HALF], heads[:, :, HALF:ROT]
                sin = cs[:, 0, tt, :].unsqueeze(1).to_broadcast([P, 2 * HEADS, HALF])
                cos = cs[:, 1, tt, :].unsqueeze(1).to_broadcast([P, 2 * HEADS, HALF])
                if tt > 0:
                    dve.wait_ge(rot_ready, TT * layer + tt)
                dve.tensor_tensor(rot[:, 0, :, :], t1, cos, ALU.mult)
                dve.tensor_tensor(rot[:, 1, :, :], t2, sin, ALU.mult)
                dve.tensor_tensor(rot[:, 2, :, :], t2, cos, ALU.mult)
                link(dve.tensor_tensor(rot[:, 3, :, :], t1, sin, ALU.mult))
                dve.tensor_tensor(t1, rot[:, 0, :, :], rot[:, 1, :, :], ALU.subtract)
                dve.tensor_tensor(t2, rot[:, 2, :, :], rot[:, 3, :, :], ALU.add).then_inc(rot_ready, 1)

            def mixer(layer):
                normalise(layer, PRE_MIX)
                if layer == 0:
                    softplus()
                for j in range(LJ):
                    dve.wait_ge(u_evac, LJ * layer + j + 1)
                    w = [pc("conv_w", (layer * LJ + j) * TAPS + t) for t in range(TAPS)]
                    link(dve.tensor_scalar(lru_y[:, j, :], u_pad[:, j, 0:T], w[0], pc("conv_b", layer * LJ + j),
                                           ALU.mult, ALU.add))
                    for t in range(1, TAPS):
                        ins = dve.scalar_tensor_tensor(out=lru_y[:, j, :], in0=u_pad[:, j, t:t + T], scalar=w[t],
                                                       in1=lru_y[:, j, :], op0=ALU.mult, op1=ALU.add)
                        if t < TAPS - 1:
                            link(ins)
                    ins.then_inc(conv_ready, 1)
                def qkv_out(m, bank):
                    dve.wait_ge(qkv_ready, 6 * layer + m + 1)
                    src = ps[bank][:, :].rearrange("p (a c) -> p a c", a=TT)
                    if m < 4:
                        return dve.tensor_copy(qk[:, :, m * 256:(m + 1) * 256], src)
                    return dve.tensor_copy(v_at[:, :, (m - 4) * 256:(m - 3) * 256], src)

                qkv_out(0, 6)
                dve.wait_ge(tau_ready, LJ * (layer + 1))
                link(dve.tensor_scalar(lru_d[:, :, :], lru_a[:, :, :], 1.0, None, ALU.add))
                dve.reciprocal(lru_d[:, :, :], lru_d[:, :, :]).then_inc(rho_ready, 1)
                link(dve.scalar_tensor_tensor(out=lru_b[:, :, :].rearrange("p a b -> p (a b)"),
                                              in0=lru_b[:, :, :].rearrange("p a b -> p (a b)"), scalar=2.0,
                                              in1=lru_y[:, :, :].rearrange("p a b -> p (a b)"),
                                              op0=ALU.mult, op1=ALU.mult))
                qkv_out(1, 7)
                dve.wait_ge(rho_ready, layer + 1)
                link(dve.tensor_tensor(lru_b[:, :, :], lru_b[:, :, :], lru_d[:, :, :], ALU.mult))
                dve.wait_ge(sqrt_ready, layer + 1)
                link(dve.tensor_tensor(lru_b[:, :, :], lru_b[:, :, :], lru_a[:, :, :], ALU.mult))
                link(dve.tensor_scalar(lru_d[:, :, :], lru_d[:, :, :], 2.0, -1.0, ALU.mult, ALU.add))
                for j in range(LJ):
                    ins = dve.tensor_tensor_scan(lru_a[:, j, :], lru_d[:, j, :], lru_b[:, j, :], 0.0,
                                                 ALU.mult, ALU.add)
                link(ins)
                dve.wait_ge(gelu_ready, LJ * (layer + 1))
                dve.tensor_tensor(lru_y[:, :, :], lru_a[:, :, :], lru_g[:, :, :], ALU.mult).then_inc(rec_ready, 1)
                qkv_out(2, 0)
                link(qkv_out(3, 1))
                for tt in range(TT):
                    if layer == 0:
                        dve.wait_ge(cs_ready, 1)
                    rotate(layer, tt)
                for m in range(2):
                    qkv_out(4 + m, 2 + m).then_inc(v_evac, 1)
                dve.wait_ge(rmsR_ready, layer + 1)
                link(dve.reciprocal(lru_b[:, 1, :], lru_b[:, 0, :]))
                for j in range(LJ):
                    ins = dve.scalar_tensor_tensor(out=lru_y[:, j, :], in0=lru_y[:, j, :],
                                                   scalar=pc("lru_out_g", layer * LJ + j), in1=lru_b[:, 1, :],
                                                   op0=ALU.mult, op1=ALU.mult)
                ins.then_inc(mixR_ready, 1)
                for b, bank in ((1, 7), (3, 1)):
                    dve.wait_ge(qk_tr, 4 * layer + b + 1)
                    dve.tensor_copy(qkT[:, 2 * b:2 * b + 2, :],
                                    ps[bank][:, :].rearrange("p (a t) -> p a t", a=2)).then_inc(qkT_dve, 1)

                def mask_head(h):
                    dve.wait_ge(scores_ready, HEADS * layer + h + 1)
                    if h >= 2:
                        dve.wait_ge(probs_ready, HEADS * layer + h - 1)
                    dve.tensor_tensor_reduce(masked[:, h % 2, 0:P], ps[h % 2][:, 0:P], cc("mask", P, T), 1.0, 3 * NEG,
                                             ALU.add, ALU.max, negmax[:, h % 2, 0:1])
                    link(dve.tensor_tensor_reduce(masked[:, h % 2, P:3 * P], ps[h % 2][:, P:3 * P], cc("mask"), 1.0,
                                                  3 * NEG, ALU.add, ALU.max, negmax[:, h % 2, 1:2]))
                    dve.tensor_scalar(negmax[:, h % 2, 2:4], negmax[:, h % 2, 0:2], -SCALE, None,
                                      ALU.mult).then_inc(masked_ready, 1)

                def turned(h):
                    dve.wait_ge(probs_tr, HEADS * layer + h + 1)
                    if h >= 2:
                        dve.wait_ge(pv_done, HEADS * layer + h - 1)
                    dve.tensor_copy(probsT[:, h % 2, :], ps[2 + h % 2][:, 0:3 * P]).then_inc(probsT_ready, 1)

                for h in range(HEADS + 1):
                    if h < HEADS:
                        mask_head(h)
                    if h >= 1:
                        turned(h - 1)
                dve.wait_ge(probs_ready, HEADS * (layer + 1))
                link(dve.reciprocal(rden[:, :, :], den[:, :, :]))
                dve.wait_ge(pv_done, HEADS * (layer + 1))
                for tt in range(TT):
                    dve.tensor_tensor(o_at[:, tt, :].rearrange("p (h d) -> p h d", d=DH),
                                      ps[6 + tt][:, :].rearrange("p (h d) -> p h d", d=DH),
                                      rden[:, :, tt:tt + 1].to_broadcast([P, HEADS, DH]),
                                      ALU.mult).then_inc(o_ready, 1)
                for tt in range(TT):
                    r = stat(layer, ATTN, tt)
                    dve.wait_ge(rstd_ready, r + 1)
                    dve.tensor_scalar(o_at[:, tt, :], o_at[:, tt, :], rstd[:, r:r + 1], None,
                                      ALU.mult).then_inc(on_ready, 1)
                dve.wait_ge(o_tr, 2 * layer + 1)
                for k in (0, 1):
                    ins = dve.tensor_scalar(mixA[:, k, :], ps[0][:, k * T:(k + 1) * T],
                                            pc("attn_out_g", layer * LJ + k), None, ALU.mult)
                ins.then_inc(mixA_dve, 1)
                post_norm(layer, POST_MIX, None, from_banks)
                dve.wait_ge(x_updated, TT * (2 * layer + 1))
                normalise(layer, PRE_FFN)

            mixer(0)
            for ft in range(FT):
                dve.wait_ge(silu_ready, ft + 1)
                if ft >= 4:
                    dve.wait_ge(down_step, ft - 3)
                dve.tensor_tensor(act[:, ft % 4, :], silu[:, ft % 2, :], ps[ft % 2][:, T:2 * T],
                                  ALU.mult).then_inc(act_ready, 1)
            post_norm(0, POST_FFN, None, from_banks)
            dve.wait_ge(x_updated, TT * 2)
            mixer(1)

            dve.memset(y_sum[:, :, :], 0.0).then_inc(comb_added, 1)
            dve.memset(item_slot[:, :, :], -1.0)
            link(dve.memset(item_gate[:, :, :], 0.0))
            dve.wait_ge(logits_ready, 1)
            link(dve.tensor_copy(lg[:, 0, :, :], ps[0][:, 0:TT * EXPERTS].rearrange("p (t e) -> p t e", t=TT)))

            def col(i):
                return top[:, i, :].unsqueeze(2).to_broadcast([P, TT, EXPERTS])

            first = cc("first").unsqueeze(1).to_broadcast([P, TT, EXPERTS])

            def one_hot(logits, best, dst):
                link(dve.tensor_reduce(top[:, best, :], logits, AX_X, ALU.max))
                link(dve.tensor_tensor(lg[:, 4, :, :], logits, col(best), ALU.is_equal))
                link(dve.tensor_tensor(lg[:, 4, :, :], lg[:, 4, :, :], first, ALU.mult))
                link(dve.tensor_reduce(top[:, 4, :], lg[:, 4, :, :], AX_X, ALU.max))
                link(dve.tensor_tensor(dst, lg[:, 4, :, :], col(4), ALU.is_equal))

            one_hot(lg[:, 0, :, :], 0, lg[:, 1, :, :])
            link(dve.scalar_tensor_tensor(out=lg[:, 2, :, :], in0=lg[:, 1, :, :], scalar=NEG, in1=lg[:, 0, :, :],
                                          op0=ALU.mult, op1=ALU.add))
            one_hot(lg[:, 2, :, :], 1, lg[:, 3, :, :])
            dve.tensor_tensor(mask_te[:, :, :], lg[:, 1, :, :], lg[:, 3, :, :], ALU.add).then_inc(mask_ready, 1)
            dve.tensor_tensor(top[:, 2, :], top[:, 1, :], top[:, 0, :], ALU.subtract).then_inc(top_diff, 1)
            dve.wait_ge(exp_diff, 1)
            link(dve.tensor_scalar(top[:, 4, :], top[:, 3, :], 1.0, None, ALU.add))
            link(dve.reciprocal(top[:, 5, :], top[:, 4, :]))
            link(dve.tensor_tensor(top[:, 4, :], top[:, 3, :], top[:, 5, :], ALU.mult))
            dve.tensor_tensor(lg[:, 4, :, :], lg[:, 1, :, :], col(5), ALU.mult)
            link(dve.tensor_tensor(lg[:, 5, :, :], lg[:, 3, :, :], col(4), ALU.mult))
            link(dve.tensor_tensor(gates[:, :, :], lg[:, 4, :, :], lg[:, 5, :, :], ALU.add))
            dve.wait_ge(slots_mm, 1)
            dve.wait_ge(mask_ready, 1)
            dve.tensor_copy(cnt[:, :], ps[1][:, 2 * EXPERTS:3 * EXPERTS])
            link(dve.tensor_tensor(slot[:, :, :], ps[1][:, 0:TT * EXPERTS].rearrange("p (t e) -> p t e", t=TT),
                                   mask_te[:, :, :], ALU.mult))
            link(dve.tensor_scalar(slot[:, :, :], slot[:, :, :], -1.0, None, ALU.add))
            dve.tensor_copy(item_slot[:, :, 0:EXPERTS], slot[:, :, :])
            link(dve.tensor_copy(item_gate[:, :, 0:EXPERTS], gates[:, :, :]))

            def one_hots(dst, item, gated, done):
                for tt in range(TT):
                    g = item_gate[:, tt, bass.ds(item, 1)] if gated else None
                    ins = dve.tensor_scalar(dst[:, tt, :], cc("iota", 0, C), item_slot[:, tt, bass.ds(item, 1)], g,
                                            ALU.is_equal, *([ALU.mult] if gated else []))
                ins.then_inc(done, 1)

            one_hots(pick, 0, False, pick_ready)

            def heT_out(b):
                g0 = PAR["pre_ffn_g"][0] + DK
                g = par[:, g0 + 4 * b:g0 + 4 * b + 4].unsqueeze(2).to_broadcast([P, 4, C])
                dve.tensor_tensor(heT[:, 4 * b:4 * b + 4, :], ps[6 + b][:, 0:4 * C].rearrange("p (k c) -> p k c", k=4),
                                  g, ALU.mult).then_inc(heT_ready, 1)

            for b in range(2):
                dve.wait_ge(gathered, b + 1)
                heT_out(b)

            for m in range(NCHUNK - 1):
                ins = dve.tensor_scalar(cand[:, 0, m * EXPERTS:(m + 1) * EXPERTS], cnt[:, :], float((m + 1) * C), None,
                                        ALU.is_gt)
            link(ins)
            link(dve.tensor_tensor_scan(cand[:, 1, :], ones[:, 0:NCAND], cand[:, 0, :], 0.0, ALU.mult, ALU.add))
            dve.tensor_copy(extra_f[:, 0:1], cand[:, 1, NCAND - 1:NCAND])
            link(dve.tensor_tensor(cand[:, 2, :], cand[:, 1, :], cand[:, 0, :], ALU.mult))
            for j in range(NEXTRA):
                link(dve.tensor_scalar(cand[:, 3, :], cand[:, 2, :], float(j + 1), None, ALU.is_equal))
                link(dve.tensor_tensor_reduce(cand[:, 4, :], cand[:, 3, :], cc("cand_e"), 1.0, 0.0, ALU.mult, ALU.add,
                                              extra_f[:, j + 1:j + 2]))
                for tt in range(TT):
                    for m in range(NCHUNK - 1):
                        cols = slice(m * EXPERTS, (m + 1) * EXPERTS)
                        dve.scalar_tensor_tensor(out=cand[:, 4, cols], in0=slot[:, tt, :], scalar=float(-(m + 1) * C),
                                                 in1=cand[:, 3, cols], op0=ALU.add, op1=ALU.mult)
                        ins = dve.tensor_tensor(cand[:, 5, cols], gates[:, tt, :], cand[:, 3, cols], ALU.mult)
                    link(ins)
                    dve.tensor_reduce(item_slot[:, tt, EXPERTS + j:EXPERTS + j + 1], cand[:, 4, :], AX_X, ALU.add)
                    link(dve.tensor_reduce(item_gate[:, tt, EXPERTS + j:EXPERTS + j + 1], cand[:, 5, :], AX_X, ALU.add))
            dve.tensor_copy(extra_i[:, :], extra_f[:, :]).then_inc(routed, 1)

            dve.wait_ge(routed, 1)
            extras = dve.value_load(extra_i[0:1, 0:1], min_val=0, max_val=NEXTRA)
            with dve.Fori(0, extras + EXPERTS) as item:
                base = item * FT + F_MOE
                for ft in range(FT):
                    dve.wait_ge(silu_ready, base + (ft + 1))
                    dve.wait_ge(down_step, base + (ft - 3))
                    dve.tensor_tensor(act[:, ft % 4, 0:C], silu[:, ft % 2, 0:C], ps[ft % 2][:, T:T + C],
                                      ALU.mult).then_inc(act_ready, 1)
                    if ft == 3:
                        dve.wait_ge(gathered, item * 2 + 2)
                        one_hots(pick_g, item, True, pick_g_ready)
                    if ft == 16:
                        dve.wait_ge(gathered, item * 2 + 2)
                        one_hots(pick, item + 1, False, pick_ready)
                dve.wait_ge(down_step, base + FT)
                dve.tensor_copy(ye[0:C, 0:512], ps[2][0:C, :]).then_inc(ye_dve, 1)
                for b in range(2):
                    dve.wait_ge(gathered, item * 2 + (3 + b))
                    heT_out(b)
                for o in range(4):
                    tt, half = o // 2, o % 2
                    dst = y_sum[:, tt, half * 512:(half + 1) * 512]
                    dve.wait_ge(comb_ready, item * 4 + (o + 1))
                    dve.tensor_tensor(dst, dst, ps[4 + o % 2][:, :], ALU.add).then_inc(comb_added, 1)
            dve.wait_ge(comb_added, (extras + EXPERTS) * 4 + 1)
            post_norm(1, POST_FFN, None, lambda tt, half: y_sum[:, tt, half * 512:(half + 1) * 512])


def kernel(**inputs):
    import concourse.bacc as bacc
    from concourse.bass_utils import run_bass_kernel_spmd

    a = {k: np.asarray(v) for k, v in inputs.items()}
    keep = np.ascontiguousarray

    def per_partition(v, pieces):
        return v.reshape(LAYERS, pieces, P).transpose(2, 0, 1).reshape(P, LAYERS * pieces)

    parts = {n: per_partition(a[n], DK if n.startswith("pre_") else LJ)
             for n, _ in PARAM_COLS if n not in ("conv_w", "router_w")}
    parts["conv_w"] = a["conv_w"].reshape(LAYERS, TAPS, LJ, P).transpose(3, 0, 2, 1).reshape(P, -1)
    parts["router_w"] = a["router_w"].reshape(DK, P, EXPERTS).transpose(1, 0, 2).reshape(P, -1)

    def columns_in_units(w):
        n, _, cols = w.shape
        return keep(w.reshape(n, DK, P, cols // FC, FC).transpose(0, 3, 2, 1, 4).reshape(n, cols // FC, P, UCOLS))

    def rows_in_units(w):
        n, rows, _ = w.shape
        return keep(w.reshape(n, rows // 256, 2, P, D).transpose(0, 1, 3, 2, 4).reshape(n, rows // 256, P, UCOLS))

    def gate_block(w):
        return w.reshape(LAYERS, LJ, 2, 64, 64).transpose(0, 2, 3, 1, 4)

    arrays = {
        "x": keep(a["x"].reshape(TT, P, D)),
        "positions": keep(a["positions"].reshape(TT, P).transpose(1, 0)),
        "consts": constants(),
        "params": keep(np.concatenate([parts[n] for n, _ in PARAM_COLS], axis=1)),
        "gains": keep(np.stack([a["post_mix_g"], a["post_ffn_g"]], axis=1)),
        "gate_blocks": keep(np.stack([gate_block(a["w_rgate"]), gate_block(a["w_igate"])], axis=3)),
        "in_units": columns_in_units(a["w_in"]),
        "out_units": rows_in_units(a["w_out"]),
        "dense_gate": columns_in_units(a["dense_w_gate"])[0],
        "dense_up": columns_in_units(a["dense_w_up"])[0],
        "dense_down": rows_in_units(a["dense_w_down"])[0],
        "moe_gate": columns_in_units(a["moe_w_gate"][0]),
        "moe_up": columns_in_units(a["moe_w_up"][0]),
        "moe_down": rows_in_units(a["moe_w_down"][0]),
    }
    nc = bacc.Bacc("TRN2", target_bir_lowering=False, num_devices=1)
    args = {n: nc.dram_tensor(n, v.shape, mybir.dt.from_np(v.dtype), kind="ExternalInput").ap()
            for n, v in arrays.items()}
    args["out"] = nc.dram_tensor("out", (TT, P, D), F32, kind="ExternalOutput").ap()
    build(nc, **args)
    r = run_bass_kernel_spmd(nc, [arrays], core_ids=[0])
    return r.results[0]["out"].reshape(1, T, D)
```

```python
from contextlib import ExitStack
import math

import numpy as np
import concourse.bass as bass
from concourse import mybir

F32 = mybir.dt.float32
F32R = mybir.dt.float32r
I32 = mybir.dt.int32
ALU = mybir.AluOpType
ACT = mybir.ActivationFunctionType
AX_X = mybir.AxisListType.X

P = 128
T = 256
TT = T // P
D = 1024
DK = D // P
LAYERS = 2
HEADS, DH = 8, 64
AW = HEADS * DH
LW = 512
LJ = LW // P
ROT = DH // 4
HALF = ROT // 2
TAPS = 4
FF = 3584
EXPERTS = 8
EPS = 1e-6
NEG = -1e30
SCALE = 1.0 / math.sqrt(DH)

UCOLS = 2048
HCOLS = UCOLS // 2
RING = 7
AHEAD = 6
FC = UCOLS // DK
NCH = FF // FC
FPC = FC // P
EC = 512
ENC = FF // EC
ETC = EC // P

C = 128
NCHUNK = -(-T // C)
NCAND = (NCHUNK - 1) * EXPERTS
NEXTRA = (2 * T - 1) // C
NITEM = EXPERTS + NEXTRA

IN_ORDER = [6, 7, 8, 9, 0, 1, 2, 3, 4, 5]
OUT_ORDER = [2, 3, 0, 1]


def dense_units():
    order = [("gate", 0), ("up", 0)]
    for c in range(1, NCH):
        order += [("gate", c), ("up", c), ("down", c - 1)]
    return order + [("down", NCH - 1)]


def expert_units():
    def two(kind, c):
        return [(kind, c, 0), (kind, c, 1)]

    order = two("gate", 0) + two("up", 0)
    for c in range(1, ENC):
        order += two("gate", c) + two("up", c) + two("down", c - 1)
    return order + two("down", ENC - 1)


DENSE_UNITS = dense_units()
EXPERT_UNITS = expert_units()
NEU = len(EXPERT_UNITS)
PRE = []
for _l in range(LAYERS):
    PRE += [("in", _l, i) for i in range(len(IN_ORDER))]
    PRE += [("out", _l, i) for i in range(len(OUT_ORDER))]
    if _l == 0:
        PRE += [(kind, 0, c) for kind, c in DENSE_UNITS]
NPRE = len(PRE)
assert NEU % RING == 0 and (2 * NEU) % AHEAD == 0
PRE_AT = {u: n for n, u in enumerate(PRE)}

PARAM_COLS = [("conv_w", LAYERS * LJ * TAPS),
              ("conv_b", LAYERS * LJ), ("b_rgate", LAYERS * LJ), ("b_igate", LAYERS * LJ),
              ("lru_lambda", LAYERS * LJ), ("attn_out_g", LAYERS * LJ), ("lru_out_g", LAYERS * LJ),
              ("router_w", DK * EXPERTS)]
CONST_COLS = [("ident", P), ("tri", P), ("iota", P), ("mask", T), ("inv_freq", HALF),
              ("first", EXPERTS), ("chunk0", NCAND), ("cand_e", NCAND)]


def columns(table):
    at, out = 0, {}
    for name, n in table:
        out[name] = (at, at + n)
        at += n
    return out, at


PAR, NPAR = columns(PARAM_COLS)
CON, NCON = columns(CONST_COLS)


def constants():
    c = np.zeros((P, NCON), np.float32)
    p = np.arange(P)[:, None]

    def put(name, v):
        a, b = CON[name]
        c[:, a:b] = v

    put("ident", p == np.arange(P)[None, :])
    put("tri", p <= np.arange(P)[None, :])
    put("iota", np.arange(P)[None, :])
    delta = p + P - np.arange(T)[None, :]
    count = ((delta >= 0) & (delta <= 128)) * 1
    count = count + ((delta >= 0) & (delta % 4 == 0)) + ((delta >= 0) & (delta % 16 == 0))
    put("mask", np.where(count > 0, np.log(np.maximum(count, 1)) / SCALE, NEG))
    put("inv_freq", 500000.0 ** (-np.arange(HALF) / HALF))
    put("first", EXPERTS - np.arange(EXPERTS)[None, :])
    put("chunk0", (np.arange(NCAND) // EXPERTS + 1)[None, :] * C)
    put("cand_e", (np.arange(NCAND) % EXPERTS)[None, :])
    return c


PRE_MIX, ATTN, POST_MIX, PRE_FFN, POST_FFN = range(5)


def stat(layer, which, tt):
    return (layer * 5 + which) * TT + tt


def build(nc, x, positions, consts, params, gains, gate_blocks, in_units, out_units,
          dense_gate, dense_up, dense_down, moe_gate, moe_up, moe_down, out):
    with ExitStack() as ctx:
        def sb(name, shape, dt=F32):
            return ctx.enter_context(nc.sbuf_tensor(name, shape, dt))

        def sem(name):
            return ctx.enter_context(nc.semaphore(name))

        ring = sb("ring", [P, RING, UCOLS])
        w_hi = sb("w_hi", [P, AHEAD, HCOLS], F32R)
        w_lo = sb("w_lo", [P, AHEAD, HCOLS], F32R)
        xs = sb("xs", [P, TT, D])
        hn = sb("hn", [P, TT, D])
        hT_hi = sb("hT_hi", [P, DK, T], F32R)
        hT_lo = sb("hT_lo", [P, DK, T], F32R)
        gain = sb("gain", [P, 3, D])
        qk = sb("qk", [P, TT, 2 * AW])
        y_sum = sb("y_sum", [P, TT, D])
        u_pad = sb("u_pad", [P, LJ, T + TAPS - 1])
        lru_y = sb("lru_y", [P, LJ, T])
        lru_a = sb("lru_a", [P, LJ, T])
        lru_b = sb("lru_b", [P, LJ, T])
        lru_d = sb("lru_d", [P, LJ, T])
        lru_g = sb("lru_g", [P, LJ, T])
        act_hi = sb("act_hi", [P, 4, T], F32R)
        act_lo = sb("act_lo", [P, 4, T], F32R)
        blocks = sb("blocks", [P, 2, LJ, P])
        con = sb("con", [P, NCON])
        par = sb("par", [P, NPAR])
        rw_hi = sb("rw_hi", [P, DK, EXPERTS], F32R)
        rw_lo = sb("rw_lo", [P, DK, EXPERTS], F32R)
        ones = sb("ones", [P, P])
        pos_i = sb("pos_i", [P, TT], I32)
        small = sb("small", [P, 4, TT, HALF])
        cs = sb("cs", [P, 2, TT, HALF])
        sp = sb("sp", [P, 4, LAYERS * LJ])
        negmax = sb("negmax", [P, 2, 4])
        den = sb("den", [P, HEADS, TT])
        rden = sb("rden", [P, HEADS, TT])
        ssq = sb("ssq", [P, 10 * LAYERS])
        ms = sb("ms", [P, 10 * LAYERS])
        rstd = sb("rstd", [P, 10 * LAYERS])
        mhalf = sb("mhalf", [P, 1])
        eps = sb("eps", [P, 1])
        lg = sb("lg", [P, 6, TT, EXPERTS])
        top = sb("top", [P, 6, TT])
        gates = sb("gates", [P, TT, EXPERTS])
        mask_te = sb("mask_te", [P, TT, EXPERTS])
        slot = sb("slot", [P, TT, EXPERTS])
        cnt = sb("cnt", [P, EXPERTS])
        cand = sb("cand", [P, 6, NCAND])
        item_slot = sb("item_slot", [P, TT, NITEM + 1])
        item_gate = sb("item_gate", [P, TT, NITEM + 1])
        extra_f = sb("extra_f", [P, 1 + NEXTRA])
        extra_i = sb("extra_i", [P, 1 + NEXTRA], I32)

        def flat(t):
            return t[:, :, :].rearrange("p a b -> p (a b)")

        v_at = hn[:, :, 0:AW]
        o_at = hn[:, :, AW:2 * AW]
        rot = flat(lru_g)[:, 0:4 * 2 * HEADS * HALF].rearrange("p (a h d) -> p a h d", a=4, d=HALF)
        masked = flat(lru_d)[:, 0:6 * P].rearrange("p (a c) -> p a c", a=2)
        probs = flat(lru_g)[:, 0:6 * P].rearrange("p (a c) -> p a c", a=2)
        probsT = flat(lru_a)[:, 0:6 * P].rearrange("p (a c) -> p a c", a=2)
        junk = flat(lru_b)
        silu = flat(lru_a).rearrange("p (a c) -> p a c", a=2)
        prod = flat(lru_b).rearrange("p (a c) -> p a c", a=2)
        ye = flat(lru_d)
        pick = flat(lru_g)[:, 0:TT * C].rearrange("p (t c) -> p t c", t=TT)
        pick_g = flat(lru_g)[:, TT * C:2 * TT * C].rearrange("p (t c) -> p t c", t=TT)
        pick_gT = flat(lru_g)[:, 2 * TT * C:2 * TT * C + T]
        q_hi, k_hi = act_hi, act_lo
        q_lo, k_lo = hT_lo[:, 0:LJ, :], hT_hi[:, 0:LJ, :]

        psum = ctx.enter_context(nc.psum_tensor("psum", [P, 8, 512], F32))
        ps = [psum[:, i, :] for i in range(8)]
        NORM_BANKS = (0, 1, 6, 7)

        def cc(name, a=None, b=None):
            lo, hi = CON[name]
            return con[:, lo + (a or 0):(lo + b) if b is not None else hi]

        def pc(name, i):
            lo, _ = PAR[name]
            return par[:, lo + i:lo + i + 1]

        ident = cc("ident")

        x_loaded = [sem(f"x_loaded{i}") for i in range(TT)]
        consts_loaded = sem("consts_loaded")
        params_loaded = sem("params_loaded")
        pos_loaded = sem("pos_loaded")
        pre_gain_loaded = sem("pre_gain_loaded")
        gain_loaded = sem("gain_loaded")
        blocks_loaded = [sem(f"blocks_loaded{i}") for i in range(2)]
        unit_loaded = [sem(f"unit_loaded{i}") for i in range(RING)]
        hi_ready = sem("hi_ready")
        lo_ready = sem("lo_ready")
        half_done = sem("half_done")
        cleared = sem("cleared")
        sumsq_ready = sem("sumsq_ready")
        pool_chain = sem("pool_chain")
        rstd_ready = sem("rstd_ready")
        hn_ready = sem("hn_ready")
        norm_tr = sem("norm_tr")
        hT_hi_ready = sem("hT_hi_ready")
        hT_ready = sem("hT_ready")
        angles_ready = sem("angles_ready")
        cs_ready = sem("cs_ready")
        explam_ready = sem("explam_ready")
        sp_ready = sem("sp_ready")
        rw_hi_ready = sem("rw_hi_ready")
        u_evac = sem("u_evac")
        conv_ready = sem("conv_ready")
        gelu_ready = sem("gelu_ready")
        gates_mm = sem("gates_mm")
        sigmoids = sem("sigmoids")
        decay_ready = sem("decay_ready")
        tanh_ready = sem("tanh_ready")
        sqrt_ready = sem("sqrt_ready")
        rec_ready = sem("rec_ready")
        rec2_ready = sem("rec2_ready")
        ssR_ready = sem("ssR_ready")
        rmsR_ready = sem("rmsR_ready")
        mixR_f32 = sem("mixR_f32")
        mixR_hi = sem("mixR_hi")
        mixR_ready = sem("mixR_ready")
        qk_evac = sem("qk_evac")
        v_evac = sem("v_evac")
        rot_ready = sem("rot_ready")
        qk_tr = sem("qk_tr")
        qkT_hi_ready = sem("qkT_hi_ready")
        qkT_ready = sem("qkT_ready")
        scores_ready = sem("scores_ready")
        masked_ready = sem("masked_ready")
        probs_ready = sem("probs_ready")
        probs_tr = sem("probs_tr")
        probsT_ready = sem("probsT_ready")
        pv_done = sem("pv_done")
        o_ready = sem("o_ready")
        on_ready = sem("on_ready")
        o_tr = sem("o_tr")
        mixA_hi = sem("mixA_hi")
        mixA_ready = sem("mixA_ready")
        tile0_done = sem("tile0_done")
        x_updated = sem("x_updated")
        silu_ready = sem("silu_ready")
        prod_ready = sem("prod_ready")
        prod_tr = sem("prod_tr")
        act_hi_ready = sem("act_hi_ready")
        act_ready = sem("act_ready")
        logits_ready = sem("logits_ready")
        top_diff = sem("top_diff")
        exp_diff = sem("exp_diff")
        mask_ready = sem("mask_ready")
        slots_mm = sem("slots_mm")
        routed = sem("routed")
        pick_ready = sem("pick_ready")
        pick_g_ready = sem("pick_g_ready")
        pick_tr = sem("pick_tr")
        pick_gT_ready = sem("pick_gT_ready")
        gathered = sem("gathered")
        tok_hi_ready = sem("tok_hi_ready")
        tok_ready = sem("tok_ready")
        ye_dve = sem("ye_dve")
        ye_act = sem("ye_act")
        comb_ready = sem("comb_ready")
        comb_added = sem("comb_added")
        dve_chain = sem("dve_chain")
        stored = sem("stored")

        block = ctx.enter_context(nc.Block())

        @block.sync
        def _(sync):
            sync.dma_start(xs[:, 0, :], x[0]).then_inc(x_loaded[0], 16)
            sync.dma_start(xs[:, 1, :], x[1]).then_inc(x_loaded[1], 16)
            sync.dma_start(con[:, :], consts).then_inc(consts_loaded, 16)
            sync.dma_start(par[:, :], params).then_inc(params_loaded, 16)
            source = {"gate": dense_gate, "up": dense_up, "down": dense_down}
            for n, (kind, layer, i) in enumerate(PRE):
                if n >= RING:
                    sync.wait_ge(lo_ready, 2 * (n - RING + 1))
                if kind == "in":
                    src = in_units[layer, IN_ORDER[i]]
                elif kind == "out":
                    src = out_units[layer, OUT_ORDER[i]]
                else:
                    src = source[kind][i]
                sync.dma_start(ring[:, n % RING, :], src).then_inc(unit_loaded[n % RING], 16)

            source_e = {"gate": moe_gate, "up": moe_up, "down": moe_down}

            def item_loads(item, expert, units=EXPERT_UNITS):
                for n, (kind, c, i) in enumerate(units):
                    sync.wait_ge(lo_ready, item * (2 * NEU) + 2 * (NPRE + n - RING + 1))
                    sync.dma_start(ring[:, (NPRE + n) % RING, :],
                                   source_e[kind][expert, 2 * c + i]).then_inc(unit_loaded[(NPRE + n) % RING], 16)

            with sync.Fori(0, EXPERTS) as item:
                item_loads(item, item)
            sync.wait_ge(routed, 1)
            extras = sync.value_load(extra_i[0:1, 0:1], min_val=0, max_val=NEXTRA)
            with sync.If(extras > 0):
                with sync.Fori(0, extras) as j:
                    expert = sync.value_load(extra_i[0:1, bass.ds(j + 1, 1)], min_val=0, max_val=EXPERTS - 1)
                    item_loads(j + EXPERTS, expert)
            item_loads(extras + EXPERTS, 0, EXPERT_UNITS[:AHEAD // 2])

            for tt in range(TT):
                sync.wait_ge(x_updated, TT * (2 * LAYERS - 1) + tt + 1)
                sync.dma_start(out[tt], xs[:, tt, :]).then_inc(stored, 16)
            sync.wait_ge(stored, 16 * TT)

        @block.gpsimd
        def _(pool):
            pool.memset(mhalf[:, :], -0.5).then_inc(pool_chain, 1)
            n = 1
            for layer in range(LAYERS):
                for which in (PRE_MIX, ATTN, POST_MIX, PRE_FFN, POST_FFN):
                    width = AW if which == ATTN else D
                    for tt in range(TT):
                        r = stat(layer, which, tt)
                        pool.wait_ge(sumsq_ready, r + 1)
                        pool.tensor_scalar(ms[:, r:r + 1], ssq[:, r:r + 1], 1.0 / width, EPS,
                                           ALU.mult, ALU.add).then_inc(pool_chain, 1)
                        n += 1
                        pool.wait_ge(pool_chain, n)
                        pool.tensor_tensor(rstd[:, r:r + 1], ms[:, r:r + 1], mhalf[:, :],
                                           ALU.pow).then_inc(rstd_ready, 1)

        @block.tensor
        def _(pe):
            def product(dst, stationary, moving, start, stop):
                s_hi, s_lo = stationary
                m_hi, m_lo = moving
                pe.matmul(dst, s_hi, m_hi, start=start, stop=False)
                pe.matmul(dst, s_hi, m_lo, start=False, stop=False)
                return pe.matmul(dst, s_lo, m_hi, start=False, stop=stop)

            def half_at(h):
                return w_hi[:, h % AHEAD, :], w_lo[:, h % AHEAD, :]

            def cols(w, lo, n, width):
                return lambda k: tuple(v[:, k * width + lo:k * width + lo + n] for v in w)

            def hT(k, a=0, b=T):
                return hT_hi[:, k, a:b], hT_lo[:, k, a:b]

            def norm_transposes(layer, which):
                n = 2 * layer + (which == PRE_FFN)
                if n == 0:
                    pe.wait_ge(consts_loaded, 16)
                for tt in range(TT):
                    pe.wait_ge(hn_ready, TT * n + tt + 1)
                    for b, bank in enumerate(NORM_BANKS):
                        for k in (2 * b, 2 * b + 1):
                            mm = pe.transpose(ps[bank][:, (k % 2) * T + tt * P:(k % 2) * T + tt * P + P],
                                              hn[:, tt, k * P:(k + 1) * P], ident)
                        if tt == TT - 1:
                            mm.then_inc(norm_tr, 1)

            def norm_wait(layer, which, s):
                pe.wait_ge(hT_ready, 4 * (2 * layer + (which == PRE_FFN)) + 2 * (s + 1))

            def channels(n, bank, layer=None):
                for s in range(2):
                    if layer is not None:
                        norm_wait(layer, PRE_MIX, s)
                    pe.wait_ge(lo_ready, 2 * n + s + 1)
                    for j in range(2):
                        w = cols(half_at(2 * n + s), j * P, P, FC)
                        for k in range(4):
                            mm = product(ps[bank + j][:, 0:T], w(k), hT(4 * s + k),
                                         start=(s == 0 and k == 0), stop=(s == 1 and k == 3))
                    mm.then_inc(half_done, 1)

            def tokens(n, bank, at):
                for s in range(2):
                    pe.wait_ge(lo_ready, 2 * n + s + 1)
                    w = cols(half_at(2 * n + s), 0, FC, FC)
                    for tt in range(TT):
                        for k in range(4):
                            mm = product(ps[bank + tt][:, at * FC:(at + 1) * FC],
                                         hT(4 * s + k, tt * P, (tt + 1) * P), w(k),
                                         start=(s == 0 and k == 0), stop=(s == 1 and k == 3))
                    mm.then_inc(half_done, 1)

            def last_rows(n, stationary):
                pe.wait_ge(lo_ready, 2 * n + 2)
                for tt in range(TT):
                    for s in range(2):
                        for half in range(2):
                            w = cols(half_at(2 * n + s), half * 512, 512, D)(0)
                            mm = product(ps[2 + 2 * tt + half], stationary(s, tt), w, start=False, stop=(s == 1))
                        if tt == TT - 1:
                            mm.then_inc(half_done, 1)
                    if tt == 0:
                        mm.then_inc(tile0_done, 1)

            def mixer(layer):
                first = PRE_AT[("in", layer, 0)]
                norm_transposes(layer, PRE_MIX)
                channels(first, 0, layer)
                channels(first + 1, 2)
                channels(first + 2, 4)
                channels(first + 3, 6)
                pe.wait_ge(u_evac, 2 * (layer + 1))
                for h in range(2):
                    pe.wait_ge(blocks_loaded[h], 16 * (layer + 1))
                for j in range(LJ):
                    pe.wait_ge(conv_ready, LJ * layer + j + 1)
                    if j >= 2:
                        pe.wait_ge(sigmoids, LJ * layer + j - 1)
                    for g in range(2):
                        mm = pe.matmul(ps[j % 2][:, g * T:(g + 1) * T], blocks[:, g, j, :], lru_y[:, j, :],
                                       start=True, stop=True)
                    mm.then_inc(gates_mm, 1)
                tokens(first + 4, 2, 0)
                tokens(first + 5, 2, 1)
                pe.wait_ge(gelu_ready, 2 * (layer + 1))
                tokens(first + 6, 6, 0)
                tokens(first + 7, 6, 1)
                tokens(first + 8, 4, 0)
                tokens(first + 9, 4, 1)
                pe.wait_ge(rec2_ready, layer + 1)
                for j in range(LJ):
                    mm = pe.matmul(ps[0][:, 0:T], ones[:, :], lru_d[:, j, :], start=(j == 0), stop=(j == LJ - 1))
                mm.then_inc(ssR_ready, 1)
                pe.wait_ge(rot_ready, TT * (layer + 1))
                for b, bank in enumerate((2, 3, 6, 7)):
                    for t in (2 * b, 2 * b + 1):
                        for tt in range(TT):
                            mm = pe.transpose(ps[bank][:, (t % 2) * T + tt * P:(t % 2) * T + tt * P + P],
                                              qk[:, tt, t * P:(t + 1) * P], ident)
                    mm.then_inc(qk_tr, 1)
                pe.wait_ge(qkT_ready, 2 * (layer + 1))
                pe.wait_ge(v_evac, layer + 1)
                pe.wait_ge(rmsR_ready, layer + 1)

                def scores(h):
                    if h >= 2:
                        pe.wait_ge(masked_ready, HEADS * layer + h - 1)
                    lo = (h % 2) * DH

                    def q(a, b):
                        return q_hi[lo:lo + DH, h // 2, a:b], q_lo[lo:lo + DH, h // 2, a:b]

                    def k(a, b):
                        return k_hi[lo:lo + DH, h // 2, a:b], k_lo[lo:lo + DH, h // 2, a:b]

                    product(ps[h % 2][:, 0:P], q(0, P), k(0, P), start=True, stop=True)
                    product(ps[h % 2][:, P:3 * P], q(P, T), k(0, T), start=True, stop=True).then_inc(scores_ready, 1)

                def turn(h):
                    pe.wait_ge(probs_ready, HEADS * layer + h + 1)
                    if h >= 2:
                        pe.wait_ge(probsT_ready, HEADS * layer + h - 1)
                    for b in range(3):
                        mm = pe.transpose(ps[2 + h % 2][:, b * P:(b + 1) * P], probs[:, h % 2, b * P:(b + 1) * P], ident)
                    mm.then_inc(probs_tr, 1)

                def weigh(h):
                    pe.wait_ge(probsT_ready, HEADS * layer + h + 1)
                    d = slice(h * DH, (h + 1) * DH)
                    pT = probsT[:, h % 2, :]
                    pe.matmul(ps[6][:, d], pT[:, 0:P], v_at[:, 0, d], start=True, stop=True)
                    pe.matmul(ps[7][:, d], pT[:, P:2 * P], v_at[:, 0, d], start=True, stop=False)
                    pe.matmul(ps[7][:, d], pT[:, 2 * P:3 * P], v_at[:, 1, d],
                              start=False, stop=True).then_inc(pv_done, 1)

                for h in range(HEADS + 2):
                    if h < HEADS:
                        scores(h)
                    if 1 <= h <= HEADS:
                        turn(h - 1)
                    if h >= 2:
                        weigh(h - 2)

                def project(n, s, k):
                    pe.wait_ge(lo_ready, 2 * n + s + 1)
                    for tt in range(TT):
                        for half in range(2):
                            w = cols(half_at(2 * n + s), half * 512, 512, D)(0)
                            mm = product(ps[2 + 2 * tt + half], hT(k, tt * P, (tt + 1) * P), w,
                                         start=(k == LJ), stop=False)
                    mm.then_inc(half_done, 1)

                pe.wait_ge(mixR_ready, layer + 1)
                for i in range(3):
                    project(first + 10 + i // 2, i % 2, LJ + i)
                pe.wait_ge(on_ready, TT * (layer + 1))
                for b in range(2):
                    for k in (2 * b, 2 * b + 1):
                        for tt in range(TT):
                            mm = pe.transpose(ps[b][:, (k % 2) * T + tt * P:(k % 2) * T + tt * P + P],
                                              o_at[:, tt, k * P:(k + 1) * P], ident)
                    mm.then_inc(o_tr, 1)
                project(first + 11, 1, LJ + 3)
                pe.wait_ge(mixA_ready, 2 * layer + 1)
                for i in range(2):
                    project(first + 12, i, i)
                pe.wait_ge(mixA_ready, 2 * (layer + 1))
                last_rows(first + 13, lambda s, tt: hT(2 + s, tt * P, (tt + 1) * P))

            def dense():
                norm_transposes(0, PRE_FFN)
                for n, (kind, c) in enumerate(DENSE_UNITS):
                    n += PRE_AT[("gate", 0, 0)]
                    bank = (0, 6)[c % 2]
                    if kind == "gate" and c >= 2:
                        pe.wait_ge(prod_ready, c - 1)
                    if kind == "down":
                        pe.wait_ge(act_ready, c + 1)
                    if (kind, c) == ("down", NCH - 1):
                        f0 = FPC * (c % 2)
                        last_rows(n, lambda s, tt: (act_hi[:, f0 + s, tt * P:(tt + 1) * P],
                                                    act_lo[:, f0 + s, tt * P:(tt + 1) * P]))
                        continue
                    for s in range(2):
                        if (kind, c) == ("gate", 0):
                            norm_wait(0, PRE_FFN, s)
                        pe.wait_ge(lo_ready, 2 * n + s + 1)
                        if kind == "down":
                            f = FPC * (c % 2) + s
                            for tt in range(TT):
                                a = (act_hi[:, f, tt * P:(tt + 1) * P], act_lo[:, f, tt * P:(tt + 1) * P])
                                for half in range(2):
                                    w = cols(half_at(2 * n + s), half * 512, 512, D)(0)
                                    mm = product(ps[2 + 2 * tt + half], a, w, start=(c == 0 and s == 0),
                                                 stop=False)
                        else:
                            at = T * (kind == "up")
                            for f in range(FPC):
                                w = cols(half_at(2 * n + s), f * P, P, FC)
                                for k in range(4):
                                    mm = product(ps[bank + f][:, at:at + T], w(k), hT(4 * s + k),
                                                 start=(s == 0 and k == 0), stop=(s == 1 and k == 3))
                        mm.then_inc(half_done, 1)

            mixer(0)
            dense()
            mixer(1)

            norm_transposes(1, PRE_FFN)
            norm_wait(1, PRE_FFN, 1)
            for tt in range(TT):
                for k in range(DK):
                    mm = product(ps[4][:, tt * EXPERTS:(tt + 1) * EXPERTS], hT(k, tt * P, (tt + 1) * P),
                                 (rw_hi[:, k, :], rw_lo[:, k, :]), start=(k == 0), stop=(k == DK - 1))
            mm.then_inc(logits_ready, 1)
            pe.wait_ge(mask_ready, 1)
            pe.matmul(ps[5][:, 0:EXPERTS], cc("tri"), mask_te[:, 0, :], start=True, stop=True)
            pe.matmul(ps[5][:, EXPERTS:2 * EXPERTS], ones[:, :], mask_te[:, 0, :], start=True, stop=False)
            pe.matmul(ps[5][:, EXPERTS:2 * EXPERTS], cc("tri"), mask_te[:, 1, :], start=False, stop=True)
            pe.matmul(ps[5][:, 2 * EXPERTS:3 * EXPERTS], ones[:, :], mask_te[:, 0, :], start=True, stop=False)
            pe.matmul(ps[5][:, 2 * EXPERTS:3 * EXPERTS], ones[:, :], mask_te[:, 1, :],
                      start=False, stop=True).then_inc(slots_mm, 1)

            def gather():
                for b in range(2):
                    for k in range(4):
                        for tt in range(TT):
                            mm = pe.matmul(ps[b][:, k * C:(k + 1) * C],
                                           hn[:, tt, (4 * b + k) * P:(4 * b + k + 1) * P], pick[:, tt, :],
                                           start=(tt == 0), stop=(tt == TT - 1))
                    mm.then_inc(gathered, 1)

            pe.wait_ge(pick_ready, 1)
            gather()
            pe.wait_ge(routed, 1)
            extras = pe.value_load(extra_i[0:1, 0:1], min_val=0, max_val=NEXTRA)
            with pe.Fori(0, extras + EXPERTS) as item:
                def turn_prod(c):
                    pe.wait_ge(prod_ready, item * ENC + (NCH + c + 1))
                    for f in range(ETC):
                        mm = pe.transpose(ps[6][:, f * C:(f + 1) * C], prod[:, c % 2, f * P:(f + 1) * P], ident)
                    mm.then_inc(prod_tr, 1)

                pe.wait_ge(tok_ready, item * 2 + 2)
                for n, (kind, c, i) in enumerate(EXPERT_UNITS):
                    if (kind, c, i) == ("gate", 1, 0):
                        pe.wait_ge(comb_added, item * 4 + 1)
                    if (kind, c, i) == ("up", c, 0) and c >= 1:
                        turn_prod(c - 1)
                    if (kind, c, i) == ("down", ENC - 1, 0):
                        turn_prod(ENC - 1)
                        pe.wait_ge(pick_ready, item + 2)
                        gather()
                    if kind == "down" and i == 0:
                        pe.wait_ge(act_ready, item * ENC + (NCH + c + 1))
                    for s in range(2):
                        h = 2 * (NPRE + n) + s
                        pe.wait_ge(lo_ready, item * (2 * NEU) + (h + 1))
                        if kind == "down":
                            f = 2 * i + s
                            a = (act_hi[:, f, (c % 2) * P:(c % 2 + 1) * P], act_lo[:, f, (c % 2) * P:(c % 2 + 1) * P])
                            for half in range(2):
                                w = cols(half_at(h), half * 512, 512, D)(0)
                                mm = product(ps[4 + half], a, w, start=(c == 0 and f == 0),
                                             stop=(c == ENC - 1 and f == ETC - 1))
                        else:
                            w = cols(half_at(h), 0, EC, EC)
                            for k in range(2):
                                kk = 4 * i + 2 * s + k
                                mm = product(ps[2 * (c % 2) + (kind == "up")], hT(kk, 0, C), w(k),
                                             start=(kk == 0), stop=(kk == DK - 1))
                        mm.then_inc(half_done, 1)
                    if (kind, c, i) == ("down", 0, 1):
                        pe.wait_ge(pick_g_ready, item + 1)
                        for tt in range(TT):
                            mm = pe.transpose(ps[7][:, tt * P:(tt + 1) * P], pick_g[:, tt, :], ident)
                        mm.then_inc(pick_tr, 1)
                pe.wait_ge(pick_gT_ready, item + 1)
                pe.wait_ge(ye_dve, item + 1)
                pe.wait_ge(ye_act, item + 1)
                for o, bank in enumerate((2, 3, 6, 7)):
                    tt, half = o // 2, o % 2
                    pe.matmul(ps[bank], pick_gT[:, tt * P:(tt + 1) * P],
                              ye[:, half * 512:(half + 1) * 512], start=True, stop=True).then_inc(comb_ready, 1)

        @block.scalar
        def _(act):
            act.dma_start(gain[:, 0, :], gains[0:1].partition_broadcast(P)).then_inc(pre_gain_loaded, 16)
            act.dma_start(pos_i[:, :], positions).then_inc(pos_loaded, 16)

            def load_layer(layer):
                if layer == 0:
                    act.wait_ge(cleared, 2)
                else:
                    act.wait_ge(gates_mm, LJ * layer)
                act.dma_start(gain[:, 1:3, :], gains[LAYERS * 2 + 2 * layer:LAYERS * 2 + 2 * layer + 2]
                              .partition_broadcast(P)).then_inc(gain_loaded, 16)
                for h in range(2):
                    act.dma_start(blocks[h * 64:(h + 1) * 64, :, :, h * 64:(h + 1) * 64],
                                  gate_blocks[layer, h]).then_inc(blocks_loaded[h], 16)

            def load_pre_gain(n):
                act.wait_ge(hn_ready, TT * n)
                act.dma_start(gain[:, 0, :], gains[n:n + 1].partition_broadcast(P)).then_inc(pre_gain_loaded, 16)

            split_next = [0]

            def split_hi(h, item=None):
                n = h // 2
                loaded, done = 16 * (n // RING + 1), h - AHEAD + 1
                if item is not None:
                    loaded, done = item * (16 * NEU // RING) + loaded, item * (2 * NEU) + done
                if h % 2 == 0:
                    act.wait_ge(unit_loaded[n % RING], loaded)
                if h >= AHEAD:
                    act.wait_ge(half_done, done)
                act.activation(w_hi[:, h % AHEAD, :], ring[:, n % RING, (h % 2) * HCOLS:(h % 2 + 1) * HCOLS],
                               ACT.Copy).then_inc(hi_ready, 1)

            def keep_up(units):
                while split_next[0] < 2 * units + AHEAD:
                    split_hi(split_next[0])
                    split_next[0] += 1

            def sumsq(r, rows):
                if r >= 1:
                    act.wait_ge(sumsq_ready, r)
                act.activation(junk[:, 0:rows.free_size()], rows, ACT.Square,
                               accum_out=ssq[:, r:r + 1]).then_inc(sumsq_ready, 1)

            def sumsq_x(layer, which):
                for tt in range(TT):
                    s = 2 * layer + (which == PRE_FFN)
                    if s == 0:
                        act.wait_ge(x_loaded[tt], 16)
                    else:
                        act.wait_ge(x_updated, TT * (s - 1) + tt + 1)
                    sumsq(stat(layer, which, tt), xs[:, tt, :])

            def tokens_of(tt):
                return psum[:, 2 + 2 * tt:4 + 2 * tt, :].rearrange("p a b -> p (a b)")

            def norm_hi(layer, which):
                n = 2 * layer + (which == PRE_FFN)
                for b, bank in enumerate(NORM_BANKS):
                    act.wait_ge(norm_tr, 4 * n + b + 1)
                    act.activation(hT_hi[:, 2 * b:2 * b + 2, :], ps[bank].rearrange("p (a t) -> p a t", a=2),
                                   ACT.Copy).then_inc(hT_hi_ready, 1)

            def small_functions():
                act.wait_ge(params_loaded, 16)
                a, b = PAR["router_w"]
                act.activation(rw_hi[:, :, :], par[:, a:b].rearrange("p (k e) -> p k e", k=DK),
                               ACT.Copy).then_inc(rw_hi_ready, 1)
                act.wait_ge(angles_ready, 1)
                act.activation(cs[:, :, :, :], small[:, 2:4, :, :], ACT.Sin).then_inc(cs_ready, 1)
                act.wait_ge(explam_ready, 1)
                act.activation(sp[:, 1, :], sp[:, 0, :], ACT.Exp, scale=-1.0).then_inc(explam_ready, 1)

            sumsq_x(0, PRE_MIX)

            def mixer(layer):
                first = PRE_AT[("in", layer, 0)]
                norm_hi(layer, PRE_MIX)
                keep_up(first)
                if layer == 0:
                    small_functions()
                load_pre_gain(2 * layer + 1)
                load_layer(layer)
                for i in range(2):
                    act.wait_ge(half_done, 2 * (first + i + 1))
                    act.activation(u_pad[:, 2 * i:2 * i + 2, TAPS - 1:], psum[:, 2 * i:2 * i + 2, 0:T],
                                   ACT.Copy).then_inc(u_evac, 1)
                    keep_up(first + i + 1)
                for i in range(2):
                    act.wait_ge(half_done, 2 * (first + i + 3))
                    act.activation(lru_g[:, 2 * i:2 * i + 2, :], psum[:, 4 + 2 * i:6 + 2 * i, 0:T],
                                   ACT.Gelu_apprx_tanh).then_inc(gelu_ready, 1)
                    keep_up(first + i + 3)
                act.wait_ge(sp_ready, 1)
                for j in range(LJ):
                    act.wait_ge(gates_mm, LJ * layer + j + 1)
                    bank = ps[j % 2]
                    act.activation(lru_a[:, j, :], bank[:, 0:T], ACT.Sigmoid, bias=pc("b_rgate", layer * LJ + j))
                    act.activation(lru_b[:, j, :], bank[:, T:2 * T], ACT.Sigmoid,
                                   bias=pc("b_igate", layer * LJ + j)).then_inc(sigmoids, 1)
                act.wait_ge(sigmoids, LJ * (layer + 1))
                for j in range(LJ):
                    act.activation(lru_d[:, j, :], lru_a[:, j, :], ACT.Exp,
                                   scale=sp[:, 2, layer * LJ + j:layer * LJ + j + 1]).then_inc(decay_ready, 1)
                act.wait_ge(decay_ready, LJ * (layer + 1))
                for j in range(LJ):
                    act.activation(lru_a[:, j, :], lru_a[:, j, :], ACT.Tanh,
                                   scale=sp[:, 3, layer * LJ + j:layer * LJ + j + 1]).then_inc(tanh_ready, 1)
                keep_up(first + 5)
                act.wait_ge(tanh_ready, LJ * (layer + 1))
                act.activation(lru_a[:, :, :], lru_a[:, :, :], ACT.Sqrt).then_inc(sqrt_ready, 1)
                keep_up(first + 6)
                act.wait_ge(rec_ready, layer + 1)
                act.activation(lru_d[:, :, :], lru_y[:, :, :], ACT.Square).then_inc(rec2_ready, 1)
                for i in range(7, 11):
                    keep_up(first + i)
                act.wait_ge(ssR_ready, layer + 1)
                act.activation(lru_b[:, 0, :], ps[0][:, 0:T], ACT.Sqrt, bias=eps[:, :],
                               scale=1.0 / LW).then_inc(rmsR_ready, 1)
                for i, (bank, hi) in enumerate(((2, q_hi), (6, k_hi))):
                    act.wait_ge(qk_tr, 4 * layer + 2 * (i + 1))
                    act.activation(hi[:, :, :],
                                   psum[:, bank:bank + 2, :].rearrange("p b (a t) -> p (b a) t", a=2),
                                   ACT.Copy).then_inc(qkT_hi_ready, 1)
                act.wait_ge(mixR_f32, layer + 1)
                act.activation(hT_hi[:, LJ:DK, :], lru_y[:, :, :], ACT.Copy).then_inc(mixR_hi, 1)
                for h in range(HEADS):
                    act.wait_ge(masked_ready, HEADS * layer + h + 1)
                    for tt, c in enumerate((slice(0, P), slice(P, 3 * P))):
                        ins = act.activation(probs[:, h % 2, c], masked[:, h % 2, c], ACT.Exp, scale=SCALE,
                                             bias=negmax[:, h % 2, 2 + tt:3 + tt], accum_out=den[:, h, tt:tt + 1])
                    ins.then_inc(probs_ready, 1)
                for tt in range(TT):
                    act.wait_ge(o_ready, TT * layer + tt + 1)
                    sumsq(stat(layer, ATTN, tt), o_at[:, tt, :])
                keep_up(first + 11)
                for b in range(2):
                    act.wait_ge(o_tr, 2 * layer + b + 1)
                    for k in (2 * b, 2 * b + 1):
                        ins = act.activation(hT_hi[:, k, :], ps[b][:, (k % 2) * T:(k % 2 + 1) * T], ACT.Identity,
                                             scale=pc("attn_out_g", layer * LJ + k))
                    ins.then_inc(mixA_hi, 1)
                keep_up(first + 12)
                keep_up(first + 13)
                act.wait_ge(tile0_done, 2 * layer + 1)
                sumsq(stat(layer, POST_MIX, 0), tokens_of(0))
                act.wait_ge(half_done, 2 * (first + 14))
                sumsq(stat(layer, POST_MIX, 1), tokens_of(1))
                sumsq_x(layer, PRE_FFN)
                norm_hi(layer, PRE_FFN)
                if layer + 1 < LAYERS:
                    load_pre_gain(2 * layer + 2)
                keep_up(first + 14)

            mixer(0)
            n0 = PRE_AT[("gate", 0, 0)]
            for n, (kind, c) in enumerate(DENSE_UNITS):
                if kind == "up":
                    act.wait_ge(half_done, 2 * (n0 + n + 1))
                    bank = (0, 6)[c % 2]
                    act.activation(silu[:, c % 2, :].rearrange("p (f t) -> p f t", f=FPC), psum[:, bank:bank + 2, 0:T],
                                   ACT.Silu).then_inc(silu_ready, 1)
                if n + 1 < len(DENSE_UNITS):
                    keep_up(n0 + n + 1)
                if kind == "up":
                    act.wait_ge(prod_ready, c + 1)
                    act.activation(act_hi[:, FPC * (c % 2):FPC * (c % 2 + 1), :],
                                   prod[:, c % 2, :].rearrange("p (f t) -> p f t", f=FPC),
                                   ACT.Copy).then_inc(act_hi_ready, 1)
            act.wait_ge(tile0_done, 2)
            sumsq(stat(0, POST_FFN, 0), tokens_of(0))
            act.wait_ge(half_done, 2 * (n0 + len(DENSE_UNITS)))
            sumsq(stat(0, POST_FFN, 1), tokens_of(1))
            sumsq_x(1, PRE_MIX)
            mixer(1)

            act.wait_ge(top_diff, 1)
            act.activation(top[:, 3, :], top[:, 2, :], ACT.Exp).then_inc(exp_diff, 1)

            def tok_hi(first):
                for b in range(2):
                    act.wait_ge(gathered, first + (b + 1))
                    act.activation(hT_hi[:, 4 * b:4 * b + 4, 0:C], ps[b].rearrange("p (k c) -> p k c", k=4),
                                   ACT.Copy).then_inc(tok_hi_ready, 1)

            tok_hi(0)
            act.wait_ge(routed, 1)
            extras = act.value_load(extra_i[0:1, 0:1], min_val=0, max_val=NEXTRA)
            with act.Fori(0, extras + EXPERTS) as item:
                def turned_hi(c):
                    act.wait_ge(prod_tr, item * ENC + (c + 1))
                    act.activation(act_hi[:, :, (c % 2) * P:(c % 2 + 1) * P], ps[6].rearrange("p (f c) -> p f c", f=ETC),
                                   ACT.Copy).then_inc(act_hi_ready, 1)

                for n, (kind, c, i) in enumerate(EXPERT_UNITS):
                    if kind == "up" and i == 1:
                        act.wait_ge(half_done, item * (2 * NEU) + 2 * (NPRE + n + 1))
                        act.activation(silu[:, c % 2, :], ps[2 * (c % 2)], ACT.Silu).then_inc(silu_ready, 1)
                    if kind == "gate" and i == 1 and c >= 1:
                        turned_hi(c - 1)
                    if (kind, c, i) == ("down", ENC - 2, 1):
                        turned_hi(ENC - 1)
                        tok_hi(item * 2 + 2)
                    if (kind, c, i) == ("down", 0, 1):
                        act.wait_ge(pick_tr, item + 1)
                        act.activation(pick_gT, ps[7][:, 0:T], ACT.Copy).then_inc(pick_gT_ready, 1)
                    if (kind, c, i) == ("down", ENC - 1, 1):
                        act.wait_ge(half_done, item * (2 * NEU) + 2 * (NPRE + NEU))
                        act.activation(ye[:, 512:D], ps[5], ACT.Copy).then_inc(ye_act, 1)
                    for s in range(2):
                        split_hi(2 * (NPRE + n) + s + AHEAD, item)
            act.wait_ge(comb_added, (extras + EXPERTS) * 4 + 1)
            for tt in range(TT):
                sumsq(stat(1, POST_FFN, tt), y_sum[:, tt, :])

        @block.vector
        def _(dve):
            links = [0]

            def link(ins):
                links[0] += 1
                ins.then_inc(dve_chain, 1)
                dve.wait_ge(dve_chain, links[0])

            split_next = [0]

            def split_lo(h, item=None):
                ready = h + 1 if item is None else item * (2 * NEU) + (h + 1)
                dve.wait_ge(hi_ready, ready)
                dve.tensor_tensor(w_lo[:, h % AHEAD, :],
                                  ring[:, (h // 2) % RING, (h % 2) * HCOLS:(h % 2 + 1) * HCOLS],
                                  w_hi[:, h % AHEAD, :].bitcast(F32), ALU.subtract).then_inc(lo_ready, 1)

            def keep_up(units, halves=AHEAD):
                while split_next[0] < 2 * units + halves:
                    split_lo(split_next[0])
                    split_next[0] += 1

            def minus(dst, value, hi):
                return dve.tensor_tensor(dst, value, hi.bitcast(F32), ALU.subtract)

            dve.memset(ones[:, :], 1.0).then_inc(cleared, 1)
            dve.memset(blocks[:, :, :, :], 0.0).then_inc(cleared, 1)
            dve.memset(eps[:, :], EPS)
            link(dve.memset(u_pad[:, :, 0:TAPS - 1], 0.0))
            def angles():
                dve.wait_ge(pos_loaded, 16)
                dve.wait_ge(consts_loaded, 16)
                link(dve.tensor_copy(top[:, 0, :], pos_i[:, :]))
                for tt in range(TT):
                    link(dve.tensor_scalar(small[:, 0, tt, :], cc("inv_freq"), top[:, 0, tt:tt + 1], None, ALU.mult))
                magic = 12582912.0
                link(dve.tensor_scalar(small[:, 1, :, :], small[:, 0, :, :], 1.0 / (2 * math.pi), None, ALU.mult))
                link(dve.tensor_scalar(small[:, 1, :, :], small[:, 1, :, :], magic, None, ALU.add))
                link(dve.tensor_scalar(small[:, 1, :, :], small[:, 1, :, :], magic, None, ALU.subtract))
                c1 = 6.28125
                c2 = 0.0019350051879882812
                c3 = 2 * math.pi - c1 - c2
                for c in (c1, c2, c3):
                    link(dve.scalar_tensor_tensor(out=small[:, 0, :, :], in0=small[:, 1, :, :], scalar=-c,
                                                  in1=small[:, 0, :, :], op0=ALU.mult, op1=ALU.add))
                lim = 3.1415925
                link(dve.tensor_scalar(small[:, 2, :, :], small[:, 0, :, :], -lim, lim, ALU.max, ALU.min))
                link(dve.tensor_scalar(small[:, 0, :, :], small[:, 0, :, :], math.pi / 2, None, ALU.add))
                link(dve.tensor_scalar(small[:, 1, :, :], small[:, 0, :, :], math.pi, -2 * math.pi, ALU.is_gt, ALU.mult))
                link(dve.tensor_tensor(small[:, 0, :, :], small[:, 0, :, :], small[:, 1, :, :], ALU.add))
                dve.tensor_scalar(small[:, 3, :, :], small[:, 0, :, :], -lim, lim, ALU.max,
                                  ALU.min).then_inc(angles_ready, 1)

            def router_lo():
                dve.wait_ge(rw_hi_ready, 1)
                a, b = PAR["router_w"]
                minus(rw_lo[:, :, :], par[:, a:b].rearrange("p (k e) -> p k e", k=DK), rw_hi[:, :, :])

            la, lb = PAR["lru_lambda"]
            lam = par[:, la:lb]

            def softplus_start():
                dve.wait_ge(params_loaded, 16)
                dve.scalar_tensor_tensor(out=sp[:, 0, :], in0=lam, scalar=-1.0, in1=lam, op0=ALU.mult,
                                         op1=ALU.max).then_inc(explam_ready, 1)

            def softplus():
                dve.wait_ge(explam_ready, 2)
                link(dve.tensor_scalar(sp[:, 0, :], sp[:, 1, :], 2.0, None, ALU.add))
                link(dve.reciprocal(sp[:, 0, :], sp[:, 0, :]))
                link(dve.tensor_tensor(sp[:, 0, :], sp[:, 0, :], sp[:, 1, :], ALU.mult))
                link(dve.tensor_tensor(sp[:, 1, :], sp[:, 0, :], sp[:, 0, :], ALU.mult))
                link(dve.tensor_scalar(sp[:, 2, :], sp[:, 1, :], 1.0 / 17, None, ALU.mult))
                for m in (15, 13, 11, 9, 7, 5, 3):
                    link(dve.scalar_tensor_tensor(out=sp[:, 2, :], in0=sp[:, 2, :], scalar=1.0 / m, in1=sp[:, 1, :],
                                                  op0=ALU.add, op1=ALU.mult))
                link(dve.scalar_tensor_tensor(out=sp[:, 2, :], in0=sp[:, 2, :], scalar=1.0, in1=sp[:, 0, :],
                                              op0=ALU.add, op1=ALU.mult))
                link(dve.tensor_scalar(sp[:, 1, :], lam, -1.0, 0.0, ALU.mult, ALU.max))
                link(dve.tensor_scalar(sp[:, 1, :], sp[:, 1, :], 4.0, None, ALU.mult))
                link(dve.scalar_tensor_tensor(out=sp[:, 3, :], in0=sp[:, 2, :], scalar=8.0, in1=sp[:, 1, :],
                                              op0=ALU.mult, op1=ALU.add))
                dve.tensor_scalar(sp[:, 2, :], sp[:, 3, :], -2.0, None, ALU.mult).then_inc(sp_ready, 1)


            def normalise(layer, which):
                n = 2 * layer + (which == PRE_FFN)
                dve.wait_ge(pre_gain_loaded, 16 * (n + 1))
                for tt in range(TT):
                    r = stat(layer, which, tt)
                    dve.wait_ge(rstd_ready, r + 1)
                    dve.scalar_tensor_tensor(out=hn[:, tt, :], in0=xs[:, tt, :], scalar=rstd[:, r:r + 1],
                                             in1=gain[:, 0, :], op0=ALU.mult, op1=ALU.mult).then_inc(hn_ready, 1)
                if n == 0:
                    softplus_start()
                    angles()
                for b, bank in enumerate(NORM_BANKS):
                    dve.wait_ge(hT_hi_ready, 4 * n + b + 1)
                    minus(hT_lo[:, 2 * b:2 * b + 2, :], ps[bank].rearrange("p (a t) -> p a t", a=2),
                          hT_hi[:, 2 * b:2 * b + 2, :]).then_inc(hT_ready, 1)

            def post_norm(layer, which, src):
                dve.wait_ge(gain_loaded, 16 * (layer + 1))
                g = 1 + (which == POST_FFN)
                for tt in range(TT):
                    r = stat(layer, which, tt)
                    dve.wait_ge(sumsq_ready, r + 1)
                    link(dve.tensor_tensor(hn[:, tt, :], src(tt), gain[:, g, :], ALU.mult))
                    dve.wait_ge(rstd_ready, r + 1)
                    dve.scalar_tensor_tensor(out=xs[:, tt, :], in0=hn[:, tt, :], scalar=rstd[:, r:r + 1],
                                             in1=xs[:, tt, :], op0=ALU.mult, op1=ALU.add).then_inc(x_updated, 1)

            def from_banks(tt):
                return psum[:, 2 + 2 * tt:4 + 2 * tt, :].rearrange("p a b -> p (a b)")

            def rotate(layer, tt):
                heads = qk[:, tt, :].rearrange("p (h d) -> p h d", d=DH)
                t1, t2 = heads[:, :, 0:HALF], heads[:, :, HALF:ROT]
                sin = cs[:, 0, tt, :].unsqueeze(1).to_broadcast([P, 2 * HEADS, HALF])
                cos = cs[:, 1, tt, :].unsqueeze(1).to_broadcast([P, 2 * HEADS, HALF])
                if tt > 0:
                    dve.wait_ge(rot_ready, TT * layer + tt)
                dve.tensor_tensor(rot[:, 0, :, :], t1, cos, ALU.mult)
                dve.tensor_tensor(rot[:, 1, :, :], t2, sin, ALU.mult)
                dve.tensor_tensor(rot[:, 2, :, :], t2, cos, ALU.mult)
                link(dve.tensor_tensor(rot[:, 3, :, :], t1, sin, ALU.mult))
                dve.tensor_tensor(t1, rot[:, 0, :, :], rot[:, 1, :, :], ALU.subtract)
                dve.tensor_tensor(t2, rot[:, 2, :, :], rot[:, 3, :, :], ALU.add).then_inc(rot_ready, 1)

            def mixer(layer):
                first = PRE_AT[("in", layer, 0)]
                normalise(layer, PRE_MIX)
                keep_up(first)
                if layer == 0:
                    router_lo()
                    softplus()
                for j in range(LJ):
                    dve.wait_ge(u_evac, 2 * layer + j // 2 + 1)
                    w = [pc("conv_w", (layer * LJ + j) * TAPS + t) for t in range(TAPS)]
                    link(dve.tensor_scalar(lru_y[:, j, :], u_pad[:, j, 0:T], w[0], pc("conv_b", layer * LJ + j),
                                           ALU.mult, ALU.add))
                    for t in range(1, TAPS):
                        ins = dve.scalar_tensor_tensor(out=lru_y[:, j, :], in0=u_pad[:, j, t:t + T], scalar=w[t],
                                                       in1=lru_y[:, j, :], op0=ALU.mult, op1=ALU.add)
                        if t < TAPS - 1:
                            link(ins)
                    ins.then_inc(conv_ready, 1)
                    if j % 2 == 1:
                        keep_up(first + j // 2 + 1)
                keep_up(first + 3)
                keep_up(first + 4)
                dve.wait_ge(sigmoids, LJ * (layer + 1))
                link(dve.tensor_tensor(lru_b[:, :, :], lru_b[:, :, :], lru_y[:, :, :], ALU.mult))
                dve.wait_ge(decay_ready, LJ * (layer + 1))
                link(dve.scalar_tensor_tensor(out=flat(lru_b), in0=flat(lru_d), scalar=1.0, in1=flat(lru_b),
                                              op0=ALU.add, op1=ALU.mult))
                keep_up(first + 5)
                dve.wait_ge(sqrt_ready, layer + 1)
                link(dve.tensor_tensor(lru_b[:, :, :], lru_b[:, :, :], lru_a[:, :, :], ALU.mult))
                for j in range(LJ):
                    ins = dve.tensor_tensor_scan(lru_a[:, j, :], lru_d[:, j, :], lru_b[:, j, :], 0.0,
                                                 ALU.mult, ALU.add)
                link(ins)
                dve.wait_ge(gelu_ready, 2 * (layer + 1))
                dve.tensor_tensor(lru_y[:, :, :], lru_a[:, :, :], lru_g[:, :, :], ALU.mult).then_inc(rec_ready, 1)
                keep_up(first + 6)
                dve.wait_ge(half_done, 2 * (first + 6))
                dve.tensor_copy(qk[:, :, 0:AW], psum[:, 2:4, :]).then_inc(qk_evac, 1)
                keep_up(first + 7)
                keep_up(first + 8)
                dve.wait_ge(half_done, 2 * (first + 8))
                dve.tensor_copy(qk[:, :, AW:2 * AW], psum[:, 6:8, :]).then_inc(qk_evac, 1)
                dve.wait_ge(qk_evac, 2 * (layer + 1))
                dve.wait_ge(rec_ready, layer + 1)
                for tt in range(TT):
                    if layer == 0:
                        dve.wait_ge(cs_ready, 1)
                    rotate(layer, tt)
                keep_up(first + 9)
                dve.wait_ge(half_done, 2 * (first + 10))
                dve.tensor_copy(v_at, psum[:, 4:6, :]).then_inc(v_evac, 1)
                keep_up(first + 10)
                dve.wait_ge(rmsR_ready, layer + 1)
                link(dve.reciprocal(lru_b[:, 1, :], lru_b[:, 0, :]))
                for j in range(LJ):
                    ins = dve.scalar_tensor_tensor(out=lru_y[:, j, :], in0=lru_y[:, j, :],
                                                   scalar=pc("lru_out_g", layer * LJ + j), in1=lru_b[:, 1, :],
                                                   op0=ALU.mult, op1=ALU.mult)
                ins.then_inc(mixR_f32, 1)
                for i, (bank, hi, lo) in enumerate(((2, q_hi, q_lo), (6, k_hi, k_lo))):
                    dve.wait_ge(qkT_hi_ready, 2 * layer + i + 1)
                    minus(lo[:, :, :], psum[:, bank:bank + 2, :].rearrange("p b (a t) -> p (b a) t", a=2),
                          hi[:, :, :]).then_inc(qkT_ready, 1)
                dve.wait_ge(mixR_f32, layer + 1)
                dve.wait_ge(mixR_hi, layer + 1)
                minus(hT_lo[:, LJ:DK, :], lru_y[:, :, :], hT_hi[:, LJ:DK, :]).then_inc(mixR_ready, 1)

                def mask_head(h):
                    dve.wait_ge(scores_ready, HEADS * layer + h + 1)
                    if h >= 2:
                        dve.wait_ge(probs_ready, HEADS * layer + h - 1)
                    dve.tensor_tensor_reduce(masked[:, h % 2, 0:P], ps[h % 2][:, 0:P], cc("mask", P, T), 1.0, 3 * NEG,
                                             ALU.add, ALU.max, negmax[:, h % 2, 0:1])
                    link(dve.tensor_tensor_reduce(masked[:, h % 2, P:3 * P], ps[h % 2][:, P:3 * P], cc("mask"), 1.0,
                                                  3 * NEG, ALU.add, ALU.max, negmax[:, h % 2, 1:2]))
                    dve.tensor_scalar(negmax[:, h % 2, 2:4], negmax[:, h % 2, 0:2], -SCALE, None,
                                      ALU.mult).then_inc(masked_ready, 1)

                def turned(h):
                    dve.wait_ge(probs_tr, HEADS * layer + h + 1)
                    if h >= 2:
                        dve.wait_ge(pv_done, HEADS * layer + h - 1)
                    dve.tensor_copy(probsT[:, h % 2, :], ps[2 + h % 2][:, 0:3 * P]).then_inc(probsT_ready, 1)

                for h in range(HEADS + 1):
                    if h < HEADS:
                        mask_head(h)
                    if h >= 1:
                        turned(h - 1)
                dve.wait_ge(probs_ready, HEADS * (layer + 1))
                link(dve.reciprocal(rden[:, :, :], den[:, :, :]))
                dve.wait_ge(pv_done, HEADS * (layer + 1))
                for tt in range(TT):
                    dve.tensor_tensor(o_at[:, tt, :].rearrange("p (h d) -> p h d", d=DH),
                                      ps[6 + tt].rearrange("p (h d) -> p h d", d=DH),
                                      rden[:, :, tt:tt + 1].to_broadcast([P, HEADS, DH]),
                                      ALU.mult).then_inc(o_ready, 1)
                for tt in range(TT):
                    r = stat(layer, ATTN, tt)
                    dve.wait_ge(rstd_ready, r + 1)
                    dve.tensor_scalar(o_at[:, tt, :], o_at[:, tt, :], rstd[:, r:r + 1], None,
                                      ALU.mult).then_inc(on_ready, 1)
                keep_up(first + 11)
                for b in range(2):
                    dve.wait_ge(mixA_hi, 2 * layer + b + 1)
                    for k in (2 * b, 2 * b + 1):
                        ins = dve.scalar_tensor_tensor(out=hT_lo[:, k, :], in0=ps[b][:, (k % 2) * T:(k % 2 + 1) * T],
                                                       scalar=pc("attn_out_g", layer * LJ + k),
                                                       in1=hT_hi[:, k, :].bitcast(F32),
                                                       op0=ALU.mult, op1=ALU.subtract)
                    ins.then_inc(mixA_ready, 1)
                keep_up(first + 12)
                keep_up(first + 13)
                post_norm(layer, POST_MIX, from_banks)
                dve.wait_ge(x_updated, TT * (2 * layer + 1))
                normalise(layer, PRE_FFN)
                keep_up(first + 14)

            mixer(0)
            n0 = PRE_AT[("gate", 0, 0)]
            for n, (kind, c) in enumerate(DENSE_UNITS):
                if kind == "up":
                    bank = (0, 6)[c % 2]
                    dve.wait_ge(silu_ready, c + 1)
                    two = [v[:, c % 2, :].rearrange("p (f t) -> p f t", f=FPC) for v in (prod, silu)]
                    dve.tensor_tensor(two[0], two[1], psum[:, bank:bank + 2, T:2 * T], ALU.mult).then_inc(prod_ready, 1)
                if n + 1 < len(DENSE_UNITS):
                    keep_up(n0 + n + 1)
                if kind == "up":
                    f = slice(FPC * (c % 2), FPC * (c % 2 + 1))
                    dve.wait_ge(act_hi_ready, c + 1)
                    minus(act_lo[:, f, :], two[0], act_hi[:, f, :]).then_inc(act_ready, 1)
            post_norm(0, POST_FFN, from_banks)
            dve.wait_ge(x_updated, TT * 2)
            mixer(1)

            dve.memset(y_sum[:, :, :], 0.0).then_inc(comb_added, 1)
            dve.memset(item_slot[:, :, :], -1.0)
            link(dve.memset(item_gate[:, :, :], 0.0))
            dve.wait_ge(logits_ready, 1)
            link(dve.tensor_copy(lg[:, 0, :, :], ps[4][:, 0:TT * EXPERTS].rearrange("p (t e) -> p t e", t=TT)))

            def col(i):
                return top[:, i, :].unsqueeze(2).to_broadcast([P, TT, EXPERTS])

            first = cc("first").unsqueeze(1).to_broadcast([P, TT, EXPERTS])

            def one_hot(logits, best, dst):
                link(dve.tensor_reduce(top[:, best, :], logits, AX_X, ALU.max))
                link(dve.tensor_tensor(lg[:, 4, :, :], logits, col(best), ALU.is_equal))
                link(dve.tensor_tensor(lg[:, 4, :, :], lg[:, 4, :, :], first, ALU.mult))
                link(dve.tensor_reduce(top[:, 4, :], lg[:, 4, :, :], AX_X, ALU.max))
                link(dve.tensor_tensor(dst, lg[:, 4, :, :], col(4), ALU.is_equal))

            one_hot(lg[:, 0, :, :], 0, lg[:, 1, :, :])
            link(dve.scalar_tensor_tensor(out=lg[:, 2, :, :], in0=lg[:, 1, :, :], scalar=NEG, in1=lg[:, 0, :, :],
                                          op0=ALU.mult, op1=ALU.add))
            one_hot(lg[:, 2, :, :], 1, lg[:, 3, :, :])
            dve.tensor_tensor(mask_te[:, :, :], lg[:, 1, :, :], lg[:, 3, :, :], ALU.add).then_inc(mask_ready, 1)
            dve.tensor_tensor(top[:, 2, :], top[:, 1, :], top[:, 0, :], ALU.subtract).then_inc(top_diff, 1)
            dve.wait_ge(slots_mm, 1)
            dve.wait_ge(mask_ready, 1)
            dve.tensor_copy(cnt[:, :], ps[5][:, 2 * EXPERTS:3 * EXPERTS])
            link(dve.tensor_tensor(slot[:, :, :], ps[5][:, 0:TT * EXPERTS].rearrange("p (t e) -> p t e", t=TT),
                                   mask_te[:, :, :], ALU.mult))
            link(dve.tensor_scalar(slot[:, :, :], slot[:, :, :], -1.0, None, ALU.add))
            link(dve.tensor_copy(item_slot[:, :, 0:EXPERTS], slot[:, :, :]))

            def one_hots(dst, item, gated, done):
                for tt in range(TT):
                    g = item_gate[:, tt, bass.ds(item, 1)] if gated else None
                    ins = dve.tensor_scalar(dst[:, tt, :], cc("iota", 0, C), item_slot[:, tt, bass.ds(item, 1)], g,
                                            ALU.is_equal, *([ALU.mult] if gated else []))
                ins.then_inc(done, 1)

            one_hots(pick, 0, False, pick_ready)

            dve.wait_ge(exp_diff, 1)
            link(dve.tensor_scalar(top[:, 4, :], top[:, 3, :], 1.0, None, ALU.add))
            link(dve.reciprocal(top[:, 5, :], top[:, 4, :]))
            link(dve.tensor_tensor(top[:, 4, :], top[:, 3, :], top[:, 5, :], ALU.mult))
            dve.tensor_tensor(lg[:, 4, :, :], lg[:, 1, :, :], col(5), ALU.mult)
            link(dve.tensor_tensor(lg[:, 5, :, :], lg[:, 3, :, :], col(4), ALU.mult))
            link(dve.tensor_tensor(gates[:, :, :], lg[:, 4, :, :], lg[:, 5, :, :], ALU.add))
            dve.tensor_copy(item_gate[:, :, 0:EXPERTS], gates[:, :, :])

            def tok_lo(first):
                for b in range(2):
                    dve.wait_ge(tok_hi_ready, first + (b + 1))
                    minus(hT_lo[:, 4 * b:4 * b + 4, 0:C], ps[b].rearrange("p (k c) -> p k c", k=4),
                          hT_hi[:, 4 * b:4 * b + 4, 0:C]).then_inc(tok_ready, 1)

            tok_lo(0)

            for m in range(NCHUNK - 1):
                ins = dve.tensor_scalar(cand[:, 0, m * EXPERTS:(m + 1) * EXPERTS], cnt[:, :], float((m + 1) * C), None,
                                        ALU.is_gt)
            link(ins)
            link(dve.tensor_tensor_scan(cand[:, 1, :], ones[:, 0:NCAND], cand[:, 0, :], 0.0, ALU.mult, ALU.add))
            dve.tensor_copy(extra_f[:, 0:1], cand[:, 1, NCAND - 1:NCAND])
            link(dve.tensor_tensor(cand[:, 2, :], cand[:, 1, :], cand[:, 0, :], ALU.mult))
            for j in range(NEXTRA):
                link(dve.tensor_scalar(cand[:, 3, :], cand[:, 2, :], float(j + 1), None, ALU.is_equal))
                link(dve.tensor_tensor_reduce(cand[:, 4, :], cand[:, 3, :], cc("cand_e"), 1.0, 0.0, ALU.mult, ALU.add,
                                              extra_f[:, j + 1:j + 2]))
                for tt in range(TT):
                    for m in range(NCHUNK - 1):
                        cols = slice(m * EXPERTS, (m + 1) * EXPERTS)
                        dve.scalar_tensor_tensor(out=cand[:, 4, cols], in0=slot[:, tt, :], scalar=float(-(m + 1) * C),
                                                 in1=cand[:, 3, cols], op0=ALU.add, op1=ALU.mult)
                        ins = dve.tensor_tensor(cand[:, 5, cols], gates[:, tt, :], cand[:, 3, cols], ALU.mult)
                    link(ins)
                    dve.tensor_reduce(item_slot[:, tt, EXPERTS + j:EXPERTS + j + 1], cand[:, 4, :], AX_X, ALU.add)
                    link(dve.tensor_reduce(item_gate[:, tt, EXPERTS + j:EXPERTS + j + 1], cand[:, 5, :], AX_X, ALU.add))
            dve.tensor_copy(extra_i[:, :], extra_f[:, :]).then_inc(routed, 1)


            dve.wait_ge(routed, 1)
            extras = dve.value_load(extra_i[0:1, 0:1], min_val=0, max_val=NEXTRA)
            with dve.Fori(0, extras + EXPERTS) as item:
                def turned_lo(c):
                    dve.wait_ge(act_hi_ready, item * ENC + (NCH + c + 1))
                    minus(act_lo[:, :, (c % 2) * P:(c % 2 + 1) * P], ps[6].rearrange("p (f c) -> p f c", f=ETC),
                          act_hi[:, :, (c % 2) * P:(c % 2 + 1) * P]).then_inc(act_ready, 1)

                for n, (kind, c, i) in enumerate(EXPERT_UNITS):
                    if kind == "up" and i == 1:
                        dve.wait_ge(silu_ready, item * ENC + (NCH + c + 1))
                        dve.tensor_tensor(prod[:, c % 2, :], silu[:, c % 2, :], ps[2 * (c % 2) + 1],
                                          ALU.mult).then_inc(prod_ready, 1)
                    if kind == "gate" and i == 1 and c >= 1:
                        turned_lo(c - 1)
                    if (kind, c, i) == ("gate", 1, 0):
                        dve.wait_ge(gathered, item * 2 + 2)
                        one_hots(pick_g, item, True, pick_g_ready)
                    if (kind, c, i) == ("gate", 3, 0):
                        one_hots(pick, item + 1, False, pick_ready)
                    if (kind, c, i) == ("down", ENC - 2, 1):
                        turned_lo(ENC - 1)
                        tok_lo(item * 2 + 2)
                    if (kind, c, i) == ("down", ENC - 1, 1):
                        dve.wait_ge(half_done, item * (2 * NEU) + 2 * (NPRE + NEU))
                        dve.tensor_copy(ye[:, 0:512], ps[4]).then_inc(ye_dve, 1)
                    for s in range(2):
                        split_lo(2 * (NPRE + n) + s + AHEAD, item)
                for o, bank in enumerate((2, 3, 6, 7)):
                    tt, half = o // 2, o % 2
                    dst = y_sum[:, tt, half * 512:(half + 1) * 512]
                    dve.wait_ge(comb_ready, item * 4 + (o + 1))
                    dve.tensor_tensor(dst, dst, ps[bank], ALU.add).then_inc(comb_added, 1)
            dve.wait_ge(comb_added, (extras + EXPERTS) * 4 + 1)
            post_norm(1, POST_FFN, lambda tt: y_sum[:, tt, :])


def kernel(**inputs):
    import concourse.bacc as bacc
    from concourse.bass_utils import run_bass_kernel_spmd

    a = {k: np.asarray(v) for k, v in inputs.items()}
    keep = np.ascontiguousarray

    def per_partition(v, pieces):
        return v.reshape(LAYERS, pieces, P).transpose(2, 0, 1).reshape(P, LAYERS * pieces)

    parts = {n: per_partition(a[n], LJ)
             for n, _ in PARAM_COLS if n not in ("conv_w", "router_w")}
    parts["conv_w"] = a["conv_w"].reshape(LAYERS, TAPS, LJ, P).transpose(3, 0, 2, 1).reshape(P, -1)
    parts["router_w"] = a["router_w"].reshape(DK, P, EXPERTS).transpose(1, 0, 2).reshape(P, -1)

    def columns_in_units(w):
        n, _, cols = w.shape
        return keep(w.reshape(n, DK, P, cols // FC, FC).transpose(0, 3, 2, 1, 4).reshape(n, cols // FC, P, UCOLS))

    def rows_in_units(w):
        n, rows, _ = w.shape
        return keep(w.reshape(n, rows // 256, 2, P, D).transpose(0, 1, 3, 2, 4).reshape(n, rows // 256, P, UCOLS))

    def columns_in_half_units(w):
        n, _, cols = w.shape
        w = w.reshape(n, 2, 4, P, cols // EC, EC).transpose(0, 4, 1, 3, 2, 5)
        return keep(w.reshape(n, 2 * cols // EC, P, UCOLS))

    def gate_block(w):
        return w.reshape(LAYERS, LJ, 2, 64, 64).transpose(0, 2, 3, 1, 4)

    arrays = {
        "x": keep(a["x"].reshape(TT, P, D)),
        "positions": keep(a["positions"].reshape(TT, P).transpose(1, 0)),
        "consts": constants(),
        "params": keep(np.concatenate([parts[n] for n, _ in PARAM_COLS], axis=1)),
        "gains": keep(np.concatenate([np.stack([a["pre_mix_g"], a["pre_ffn_g"]], axis=1).reshape(2 * LAYERS, D),
                                      np.stack([a["post_mix_g"], a["post_ffn_g"]], axis=1).reshape(2 * LAYERS, D)])),
        "gate_blocks": keep(np.stack([gate_block(a["w_rgate"]), gate_block(a["w_igate"])], axis=3)),
        "in_units": columns_in_units(a["w_in"]),
        "out_units": rows_in_units(a["w_out"]),
        "dense_gate": columns_in_units(a["dense_w_gate"])[0],
        "dense_up": columns_in_units(a["dense_w_up"])[0],
        "dense_down": rows_in_units(a["dense_w_down"])[0],
        "moe_gate": columns_in_half_units(a["moe_w_gate"][0]),
        "moe_up": columns_in_half_units(a["moe_w_up"][0]),
        "moe_down": rows_in_units(a["moe_w_down"][0]),
    }
    nc = bacc.Bacc("TRN2", target_bir_lowering=False, num_devices=1)
    args = {n: nc.dram_tensor(n, v.shape, mybir.dt.from_np(v.dtype), kind="ExternalInput").ap()
            for n, v in arrays.items()}
    args["out"] = nc.dram_tensor("out", (TT, P, D), F32, kind="ExternalOutput").ap()
    build(nc, **args)
    r = run_bass_kernel_spmd(nc, [arrays], core_ids=[0])
    return r.results[0]["out"].reshape(1, T, D)
```
